# Optimizing a Trainium2 kernel written in Bass

```python
import jax
import jax.numpy as jnp
from jax import lax
import numpy as np

D_MODEL = 1024
BATCH = 1
SEQ = 1024
DEPTH = 2

CTX_LEN = 256
GRID_W = 64
CHUNK = 64
EPS = 1e-6
LN_X_EPS = 64e-5

R_HEADS = 4
R_HD = 64
R_W = R_HEADS * R_HD
R_DECAY_LORA = 64
R_ICLR_LORA = 64
R_VRES_LORA = 32
T_HEADS = 4
T_HD = 64
T_W = T_HEADS * T_HD
ROPE_BASE = 10000.0
G_HEADS = 4
G_HD = 128
G_W = G_HEADS * G_HD
CONV_K = 3

D_MIX = R_W + T_W + G_W
R_SHIFT_W = 3 * R_W + R_DECAY_LORA + R_ICLR_LORA
R_IN = R_SHIFT_W + R_W
T_IN = 4 * T_W
G_IN = 4 * G_W + 4 * G_HEADS
N_IN = R_IN + T_IN + G_IN

kernel_name = "hybrid_rwkv7_retention_gdn_prefix_block"

def rms_norm(x, gain):
    xf = x.astype(jnp.float32)
    y = xf * lax.rsqrt(jnp.mean(xf * xf, axis=-1, keepdims=True) + EPS)
    return (y * gain.astype(jnp.float32)).astype(x.dtype)

def layer_norm(x, gain, bias, eps):
    xf = x.astype(jnp.float32)
    mu = jnp.mean(xf, axis=-1, keepdims=True)
    xc = xf - mu
    y = xc * lax.rsqrt(jnp.mean(xc * xc, axis=-1, keepdims=True) + eps)
    return (y * gain.astype(jnp.float32) + bias.astype(jnp.float32)).astype(x.dtype)

def l2_normalize(x):
    xf = x.astype(jnp.float32)
    return (xf * lax.rsqrt(jnp.sum(xf * xf, axis=-1, keepdims=True) + EPS)).astype(x.dtype)

def dirs_shared(z):
    return jnp.stack([z, jnp.flip(z, 1)])

def to_dirs(z):
    return jnp.stack([z[0], jnp.flip(z[1], 1)])

def from_dirs(o):
    return o[0] + jnp.flip(o[1], 1)

def q_shift_grid(z, rows):
    b, s, c = z.shape
    g = z.reshape(b, rows, GRID_W, c // 4, 4)
    from_left = jnp.pad(g[:, :, :-1, :, 0], ((0, 0), (0, 0), (1, 0), (0, 0)))
    from_right = jnp.pad(g[:, :, 1:, :, 1], ((0, 0), (0, 0), (0, 1), (0, 0)))
    from_above = jnp.pad(g[:, :-1, :, :, 2], ((0, 0), (1, 0), (0, 0), (0, 0)))
    from_below = jnp.pad(g[:, 1:, :, :, 3], ((0, 0), (0, 1), (0, 0), (0, 0)))
    return jnp.stack([from_left, from_right, from_above, from_below], -1).reshape(b, s, c)

def q_shift_seq(z):
    b, s, c = z.shape
    g = z.reshape(b, s, c // 4, 4)
    prev = jnp.pad(g[:, :-1], ((0, 0), (1, 0), (0, 0), (0, 0)))
    nxt = jnp.pad(g[:, 1:], ((0, 0), (0, 1), (0, 0), (0, 0)))
    return jnp.stack([prev[..., 0], nxt[..., 1], prev[..., 2], nxt[..., 3]], -1).reshape(b, s, c)

def depthwise_conv_centred(z, w):
    k = w.shape[0]
    return lax.conv_general_dilated(
        z, w[:, None, :].astype(z.dtype), window_strides=(1,),
        padding=[((k - 1) // 2, k // 2)], dimension_numbers=("NWC", "WIO", "NWC"),
        feature_group_count=z.shape[-1])

def axial_rope(rows):
    n_freq = T_HD // 4
    inv = ROPE_BASE ** (-jnp.arange(n_freq, dtype=jnp.float32) / n_freq)
    t = jnp.arange(rows * GRID_W)
    r = (t // GRID_W).astype(jnp.float32)
    col = (t % GRID_W).astype(jnp.float32)
    ang = jnp.concatenate([r[:, None] * inv, col[:, None] * inv], -1)
    return jnp.cos(ang), jnp.sin(ang)

def apply_rope(z, cos, sin):
    z1, z2 = jnp.split(z.astype(jnp.float32), 2, -1)
    cos, sin = cos[:, None, :], sin[:, None, :]
    return jnp.concatenate([z1 * cos - z2 * sin, z1 * sin + z2 * cos], -1).astype(z.dtype)

def rwkv7_scan(r, w, k, v, a, b, s0):
    def step(s, inp):
        r_t, w_t, k_t, v_t, a_t, b_t = inp
        sa = jnp.einsum("dbhvk,dbhk->dbhv", s, a_t)
        s = s * w_t[..., None, :] + v_t[..., :, None] * k_t[..., None, :] + sa[..., :, None] * b_t[..., None, :]
        return s, jnp.einsum("dbhvk,dbhk->dbhv", s, r_t)
    xs = tuple(jnp.moveaxis(z.astype(jnp.float32), 2, 0) for z in (r, w, k, v, a, b))
    s_fin, o = lax.scan(step, s0, xs)
    return jnp.moveaxis(o, 0, 2), s_fin

def to_chunks(z):
    d2, b, t, h, d = z.shape
    return z.astype(jnp.float32).reshape(d2, b, t // CHUNK, CHUNK, h, d).transpose(0, 1, 2, 4, 3, 5)

def from_chunks(o):
    d2, b, n, h, c, d = o.shape
    return o.transpose(0, 1, 2, 4, 3, 5).reshape(d2, b, n * c, h, d)

def retention_chunked(q, k, v, log_gamma, s0):
    qc, kc, vc = to_chunks(q), to_chunks(k), to_chunks(v)
    pos = jnp.arange(CHUNK, dtype=jnp.float32)
    lg = log_gamma.astype(jnp.float32)[:, :, None]
    rel = pos[:, None] - pos[None, :]
    causal = rel >= 0
    d_intra = jnp.where(causal, jnp.exp(lg[..., None] * jnp.where(causal, rel, 0.0)), 0.0)
    q_dec = jnp.exp(lg * (pos + 1.0))
    k_dec = jnp.exp(lg * (CHUNK - 1.0 - pos))
    c_dec = jnp.exp(lg[..., 0] * CHUNK)[:, None, :, None, None]
    scores = jnp.einsum("dbnhik,dbnhjk->dbnhij", qc, kc) * d_intra[:, None, None]
    o_intra = jnp.einsum("dbnhij,dbnhjv->dbnhiv", scores, vc)
    kv = jnp.einsum("dbnhjk,dbnhjv->dbnhkv", kc * k_dec[:, None, None, :, :, None], vc)
    qd = qc * q_dec[:, None, None, :, :, None]

    def step(s, inp):
        kv_n, qd_n = inp
        o_n = jnp.einsum("dbhik,dbhkv->dbhiv", qd_n, s)
        return c_dec * s + kv_n, o_n
    s_fin, o_inter = lax.scan(step, s0, (jnp.moveaxis(kv, 2, 0), jnp.moveaxis(qd, 2, 0)))
    return from_chunks(o_intra + jnp.moveaxis(o_inter, 0, 2)), s_fin

def gated_delta_chunked(q, k, v, g, beta, s0):
    d2, b, t, h, dk = q.shape
    n = t // CHUNK
    qc = to_chunks(q) * (dk ** -0.5)
    kc, vc = to_chunks(k), to_chunks(v)
    per_chunk = lambda z: z.astype(jnp.float32).reshape(d2, b, n, CHUNK, h).transpose(0, 1, 2, 4, 3)
    gc = jnp.cumsum(per_chunk(g), axis=-1)
    bt = per_chunk(beta)[..., None]
    pos = jnp.arange(CHUNK)
    incl = pos[:, None] >= pos[None, :]
    strict = pos[:, None] > pos[None, :]
    decay = jnp.exp(jnp.where(incl, gc[..., :, None] - gc[..., None, :], -jnp.inf))
    kb = kc * bt
    lower = jnp.where(strict, jnp.einsum("dbnhik,dbnhjk->dbnhij", kb, kc) * decay, 0.0)
    eye = jnp.eye(CHUNK, dtype=jnp.float32)
    tmat = lax.linalg.triangular_solve(eye + lower, jnp.broadcast_to(eye, lower.shape),
                                       left_side=True, lower=True, unit_diagonal=True)
    u = jnp.einsum("dbnhij,dbnhjv->dbnhiv", tmat, vc * bt)
    w = jnp.einsum("dbnhij,dbnhjk->dbnhik", tmat, kb * jnp.exp(gc)[..., None])
    a_qk = jnp.einsum("dbnhik,dbnhjk->dbnhij", qc, kc) * decay
    qg = qc * jnp.exp(gc)[..., None]
    g_last = gc[..., -1:]
    kt = kc * jnp.exp(g_last - gc)[..., None]
    cd = jnp.exp(g_last)[..., None]

    def step(s, inp):
        u_n, w_n, qg_n, a_n, kt_n, cd_n = inp
        v_new = u_n - jnp.einsum("dbhck,dbhkv->dbhcv", w_n, s)
        o_n = jnp.einsum("dbhck,dbhkv->dbhcv", qg_n, s) + jnp.einsum("dbhij,dbhjv->dbhiv", a_n, v_new)
        s = s * cd_n + jnp.einsum("dbhck,dbhcv->dbhkv", kt_n, v_new)
        return s, o_n
    xs = tuple(jnp.moveaxis(z, 2, 0) for z in (u, w, qg, a_qk, kt, cd))
    s_fin, o = lax.scan(step, s0, xs)
    return from_chunks(jnp.moveaxis(o, 0, 2)), s_fin

def rwkv7_branch(u, rows, s0, v_first, vres, mu, w0, w2, a0, a2, k_k, k_a, r_k, ln_g, ln_b):
    b, t, _ = u.shape
    f32 = jnp.float32
    pre, gate = u[..., :R_SHIFT_W], u[..., R_SHIFT_W:]
    shifted = q_shift_seq(pre) if rows is None else q_shift_grid(pre, rows)
    xs = (pre + (shifted - pre) * mu).astype(f32)
    r, k, v, wd, ad = jnp.split(xs, [R_W, 2 * R_W, 3 * R_W, 3 * R_W + R_DECAY_LORA], -1)
    if vres is not None:
        v0, v1, v2 = (p.astype(f32) for p in vres)
        v = v + (v_first.astype(f32) - v) * jax.nn.sigmoid(v0 + (v @ v1) @ v2)
    w_log = -jax.nn.softplus(-(w0.astype(f32)[:, None, None, :]
                               + jnp.einsum("btr,drc->dbtc", jnp.tanh(wd), w2.astype(f32)))) - 0.5
    decay = jnp.exp(-jnp.exp(w_log))
    iclr = jax.nn.sigmoid(a0.astype(f32)[:, None, None, :] + jnp.einsum("btr,drc->dbtc", ad, a2.astype(f32)))
    heads = lambda z: z.reshape(z.shape[:-1] + (R_HEADS, R_HD))
    kk = l2_normalize(heads(k * k_k.astype(f32)))
    k_d = heads(k * (1.0 + (iclr - 1.0) * k_a.astype(f32)))
    r_h, v_h = heads(r), heads(v)
    o, s_fin = rwkv7_scan(dirs_shared(r_h), to_dirs(heads(decay)), to_dirs(k_d), dirs_shared(v_h),
                          dirs_shared(-kk), to_dirs(kk * heads(iclr)), s0)
    o = layer_norm(from_dirs(o), ln_g.reshape(R_HEADS, R_HD), ln_b.reshape(R_HEADS, R_HD), LN_X_EPS)
    bonus = jnp.sum(r_h * k_d * r_k.astype(f32), axis=-1, keepdims=True)
    o = o + (bonus[0] + bonus[1]) * v_h
    y = o.reshape(b, t, R_W) * jax.nn.silu(gate.astype(f32))
    return y.astype(u.dtype), s_fin, v.astype(u.dtype)

def retention_branch(u, rope, s0, decay_logit, norm_g):
    b, t, _ = u.shape
    q, k, v, gate = jnp.split(u, 4, -1)
    q = q.reshape(b, t, T_HEADS, T_HD)
    k = k.reshape(b, t, T_HEADS, T_HD) * (T_HD ** -0.5)
    v = v.reshape(b, t, T_HEADS, T_HD)
    if rope is not None:
        q, k = apply_rope(q, *rope), apply_rope(k, *rope)
    log_gamma = jax.nn.log_sigmoid(decay_logit.astype(jnp.float32))
    o, s_fin = retention_chunked(dirs_shared(q), dirs_shared(k), dirs_shared(v), log_gamma, s0)
    o = rms_norm(from_dirs(o), norm_g.reshape(T_HEADS, T_HD))
    y = o.reshape(b, t, T_W) * jax.nn.silu(gate.astype(jnp.float32))
    return y.astype(u.dtype), s_fin

def gated_deltanet_branch(u, s0, conv_w, a_log, dt_bias, norm_g):
    b, t, _ = u.shape
    f32 = jnp.float32
    qkv = jax.nn.silu(depthwise_conv_centred(u[..., :3 * G_W], conv_w))
    z = u[..., 3 * G_W:4 * G_W]
    alpha_raw = jnp.moveaxis(u[..., 4 * G_W:4 * G_W + 2 * G_HEADS].reshape(b, t, 2, G_HEADS), 2, 0)
    beta_raw = jnp.moveaxis(u[..., 4 * G_W + 2 * G_HEADS:].reshape(b, t, 2, G_HEADS), 2, 0)
    q, k, v = jnp.split(qkv.reshape(b, t, 3, G_HEADS, G_HD), 3, axis=2)
    q, k, v = l2_normalize(q[:, :, 0]), l2_normalize(k[:, :, 0]), v[:, :, 0]
    g = -jnp.exp(a_log.astype(f32))[:, None, None, :] * jax.nn.softplus(
        alpha_raw.astype(f32) + dt_bias.astype(f32)[:, None, None, :])
    beta = jax.nn.sigmoid(beta_raw.astype(f32))
    o, s_fin = gated_delta_chunked(dirs_shared(q), dirs_shared(k), dirs_shared(v), to_dirs(g), to_dirs(beta), s0)
    o = rms_norm(from_dirs(o), norm_g)
    y = o.reshape(b, t, G_W) * jax.nn.silu(z.astype(f32))
    return y.astype(u.dtype), s_fin

def token_mixers(u, rows, rope, states, v_first, vres, rk_p, ret_p, gdn_p):
    u_r, u_t, u_g = jnp.split(u, [R_IN, R_IN + T_IN], -1)
    y_r, s_r, v = rwkv7_branch(u_r, rows, states[0], v_first, vres, *rk_p)
    y_t, s_t = retention_branch(u_t, rope, states[1], *ret_p)
    y_g, s_g = gated_deltanet_branch(u_g, states[2], *gdn_p)
    return jnp.concatenate([y_r, y_t, y_g], -1), (s_r, s_t, s_g), v

def setup_inputs(seed: int = 0) -> dict:
    key = jax.random.key(seed)
    ks = iter(jax.random.split(key, 40))
    f32 = jnp.float32
    nrm = lambda shape, scale: scale * jax.random.normal(next(ks), shape, f32)
    L = DEPTH
    ramp = jnp.linspace(0.0, 1.0, R_W, dtype=f32)
    ret_base = jnp.log(jnp.exp2(5.0 + jnp.arange(T_HEADS, dtype=f32)) - 1.0)
    dt = jnp.exp(jax.random.uniform(next(ks), (L, 2, G_HEADS), f32, np.log(1e-3), np.log(1e-1)))
    return {
        "x": nrm((BATCH, SEQ, D_MODEL), 1.0),
        "c": nrm((BATCH, D_MODEL), 1.0),
        "ctx": nrm((BATCH, CTX_LEN, D_MODEL), 1.0),
        "c_ctx": nrm((D_MODEL,), 1.0),
        "ada_w": nrm((L, D_MODEL, 3 * D_MODEL), 0.02),
        "ada_b": nrm((L, 3 * D_MODEL), 0.01),
        "norm_g": 1.0 + nrm((L, D_MODEL), 0.02),
        "w_in": nrm((L, D_MODEL, N_IN), D_MODEL ** -0.5),
        "w_out": nrm((L, D_MIX, D_MODEL), D_MIX ** -0.5),
        "rk_mu": jax.random.uniform(next(ks), (L, R_SHIFT_W), f32),
        "rk_w0": (-6.0 + 5.0 * ramp) + nrm((L, 2, R_W), 0.1),
        "rk_w2": nrm((L, 2, R_DECAY_LORA, R_W), 0.1 * R_DECAY_LORA ** -0.5),
        "rk_a0": nrm((L, 2, R_W), 0.1),
        "rk_a2": nrm((L, 2, R_ICLR_LORA, R_W), 0.1 * R_ICLR_LORA ** -0.5),
        "rk_kk": 0.85 + nrm((L, R_W), 0.02),
        "rk_ka": 1.0 + nrm((L, R_W), 0.02),
        "rk_rk": nrm((L, R_HEADS, R_HD), 0.1),
        "rk_v0": 1.0 + nrm((L - 1, R_W), 0.1),
        "rk_v1": nrm((L - 1, R_W, R_VRES_LORA), R_W ** -0.5),
        "rk_v2": nrm((L - 1, R_VRES_LORA, R_W), 0.1 * R_VRES_LORA ** -0.5),
        "rk_ln_g": 1.0 + nrm((L, R_W), 0.02),
        "rk_ln_b": nrm((L, R_W), 0.01),
        "ret_decay": ret_base + nrm((L, 2, T_HEADS), 0.05),
        "ret_norm_g": 1.0 + nrm((L, T_W), 0.02),
        "gdn_conv": nrm((L, CONV_K, 3 * G_W), CONV_K ** -0.5),
        "gdn_a_log": jnp.log(jax.random.uniform(next(ks), (L, 2, G_HEADS), f32, 1.0, 16.0)),
        "gdn_dt_bias": dt + jnp.log(-jnp.expm1(-dt)),
        "gdn_norm_g": 1.0 + nrm((L, G_HD), 0.02),
        "final_g": 1.0 + nrm((D_MODEL,), 0.02),
    }

def reference(x, c, ctx, c_ctx, ada_w, ada_b, norm_g, w_in, w_out, rk_mu, rk_w0, rk_w2, rk_a0, rk_a2,
              rk_kk, rk_ka, rk_rk, rk_v0, rk_v1, rk_v2, rk_ln_g, rk_ln_b, ret_decay, ret_norm_g,
              gdn_conv, gdn_a_log, gdn_dt_bias, gdn_norm_g, final_g):
    b, s, _ = x.shape
    rows = s // GRID_W
    rope = axial_rope(rows)
    f32 = jnp.float32
    zero_states = (jnp.zeros((2, b, R_HEADS, R_HD, R_HD), f32),
                   jnp.zeros((2, b, T_HEADS, T_HD, T_HD), f32),
                   jnp.zeros((2, b, G_HEADS, G_HD, G_HD), f32))
    silu_c = jax.nn.silu(c)
    silu_cc = jax.nn.silu(c_ctx)
    vf_ctx = None
    vf_lat = None
    for l in range(DEPTH):
        mod_lat = silu_c @ ada_w[l] + ada_b[l]
        mod_ctx = silu_cc @ ada_w[l] + ada_b[l]
        shift_l, scale_l, gate_l = jnp.split(mod_lat[:, None, :], 3, -1)
        shift_c, scale_c, gate_c = jnp.split(mod_ctx, 3, -1)
        h_ctx = rms_norm(ctx, norm_g[l]) * (1.0 + scale_c) + shift_c
        h_lat = rms_norm(x, norm_g[l]) * (1.0 + scale_l) + shift_l
        vres = None if l == 0 else (rk_v0[l - 1], rk_v1[l - 1], rk_v2[l - 1])
        rk_p = (rk_mu[l], rk_w0[l], rk_w2[l], rk_a0[l], rk_a2[l], rk_kk[l], rk_ka[l], rk_rk[l],
                rk_ln_g[l], rk_ln_b[l])
        ret_p = (ret_decay[l], ret_norm_g[l])
        gdn_p = (gdn_conv[l], gdn_a_log[l], gdn_dt_bias[l], gdn_norm_g[l])
        y_ctx, st_ctx, v_ctx = token_mixers(h_ctx @ w_in[l], None, None, zero_states, vf_ctx, vres,
                                            rk_p, ret_p, gdn_p)
        y_lat, _, v_lat = token_mixers(h_lat @ w_in[l], rows, rope, st_ctx, vf_lat, vres,
                                       rk_p, ret_p, gdn_p)
        if l == 0:
            vf_ctx, vf_lat = v_ctx, v_lat
        x = x + gate_l * (y_lat @ w_out[l])
        if l + 1 < DEPTH:
            ctx = ctx + gate_c * (y_ctx @ w_out[l])
    return rms_norm(x, final_g)


_drawn_inputs = setup_inputs


def setup_inputs(seed=0):
    import zlib

    import numpy as np

    out = dict(_drawn_inputs(seed))
    spreads = {}
    factors = {'ada_b': 3.558,
     'norm_g': 3.94,
     'rk_w2': 25.274,
     'rk_a0': 5.992,
     'rk_a2': 5.69,
     'rk_kk': 200.0,
     'rk_ka': 5.244,
     'rk_v0': 8.0,
     'rk_v1': 8.0,
     'rk_v2': 8.0,
     'rk_ln_g': 200.0,
     'rk_ln_b': 200.0,
     'ret_norm_g': 200.0,
     'gdn_norm_g': 64.0,
     'final_g': 2.721,
     'gdn_a_log': 3.78}
    for name, (base, spread) in spreads.items():
        noise = np.random.default_rng([zlib.crc32(name.encode()), seed]).standard_normal(out[name].shape)
        drawn = base * np.exp(spread * noise) if base else spread * noise
        out[name] = jnp.asarray(drawn.astype(out[name].dtype))
    for name, factor in factors.items():
        out[name] = (out[name] * factor).astype(out[name].dtype)
    return out
```

```python
from contextlib import ExitStack
import math

import concourse.bass as bass
import numpy as np
from concourse import mybir

F32 = mybir.dt.float32
I32 = mybir.dt.int32
ALU = mybir.AluOpType
ACT = mybir.ActivationFunctionType
AX = mybir.AxisListType.X

P = 128
D = 1024
KT = D // P
CTX = 256
SEQ = 1024
T = CTX + SEQ
CH = 128
NC_CTX = CTX // CH
NCH = T // CH
GRID = 64
DEPTH = 2
N_IN = 4240
PIECES = ((0, CTX), (CTX, 512), (CTX + 512, 512))
LEVELS = 7
EPS = 1e-6
LN_EPS = 64e-5
NEG_SQRT_E = -math.exp(-0.5)

C_IDENT, C_ONES, C_BLK, C_PERM = 0, 128, 256, 384
C_LVL = 512
C_SI = C_LVL + LEVELS * 2 * 128
C_REL = C_SI + 512
C_POSR = C_REL + 256
C_POSC = C_POSR + 256
C_TYPE = C_POSC + 2
N_CST = C_TYPE + 4

W_RK_COMMON, W_RK, W_RT, W_GD, N_WT = 0, 3, 9, 17, 33

RKC_MU, RKC_V0, RKC_V1, RKC_V2, N_RKC = 0, 3, 5, 69, 325
RKU_LORA, RKU_W0, RKU_A0, RKU_KK, RKU_KA, RKU_RK, RKU_LNG, RKU_LNB, RKU_MU, N_RKU = 0, 256, 258, 260, 261, 262, 263, 264, 265, 267
RTU_ROW, RTU_COL, RTU_G, N_RTU = 0, 4, 6, 7
GDU_CONV, GDU_G, N_GDU = 0, 18, 19
G_G, G_NGC, G_BETA, G_NEG, G_EG, G_WK, G_CD, N_GS = 0, 1, 2, 3, 4, 5, 6, 7


def constants():
    c = np.zeros((P, N_CST), np.float32)
    j, i = np.arange(P)[:, None], np.arange(P)[None, :]
    c[:, C_IDENT:C_IDENT + P] = j == i
    c[:, C_ONES:C_ONES + P] = 1
    c[:, C_BLK:C_BLK + P] = j // 64 == i // 64
    c[:, C_PERM:C_PERM + P] = np.where((i % 64 < 32) & (j == i + 32), -1, 0) + np.where((i % 64 >= 32) & (j == i - 32), 1, 0)
    for lv in range(LEVELS):
        b = 1 << lv
        same = j // (2 * b) == i // (2 * b)
        for d, (row, col) in enumerate(((j, i), (i, j))):
            block = same & (row % (2 * b) >= b) & (col % (2 * b) < b)
            at = C_LVL + (lv * 2 + d) * P
            c[:, at:at + P] = np.where(j == i, 1, 0) - np.where(block, 1, 0)
    for d, (first, then) in enumerate(((j, i), (i, j))):
        at = C_SI + d * 256
        c[:, at:at + P] = first < then
        c[:, at + P:at + 2 * P] = first <= then
        c[:, C_REL + d * P:C_REL + (d + 1) * P] = np.maximum(then - first, 0)
        c[:, C_POSR + d * P:C_POSR + (d + 1) * P] = (i + 1) if d == 0 else (P - i)
        c[:, C_POSC + d] = (P - 1 - j[:, 0]) if d == 0 else j[:, 0]
    for s in range(4):
        c[:, C_TYPE + s] = j[:, 0] % 4 == s
    return c


def rope_tables():
    n_freq = 16
    inv = np.float32(10000.0) ** (-np.arange(n_freq, dtype=np.float32) / np.float32(n_freq))
    t = np.arange(SEQ)
    ang = np.concatenate([(t // GRID).astype(np.float32)[:, None] * inv, (t % GRID).astype(np.float32)[:, None] * inv], -1)
    ang = np.concatenate([ang] * 4, -1).T
    return np.ascontiguousarray(np.stack([np.cos(ang), np.sin(ang)]).astype(np.float32))


class Stage:

    def __init__(self, nc, names):
        self.nc, self.names, self.ctx = nc, names.split(), ExitStack()

    def __enter__(self):
        self.s = {n: self.ctx.enter_context(self.nc.semaphore(n)) for n in self.names}
        self.block_guard = self.nc.Block()
        return self.block_guard.__enter__(), self.s

    def __exit__(self, *exc):
        self.block_guard.__exit__(*exc)
        if exc[0] is None:
            sems = self.s
            with self.nc.Block() as block:
                @block.sync
                def _(sp):
                    for n in sems:
                        sp.sem_clear(sems[n])
        return self.ctx.__exit__(*exc)


class Link:

    def __init__(self, eng, sem):
        self.eng, self.sem, self.n = eng, sem, 0

    def __call__(self, ins):
        ins.then_inc(self.sem, 1)
        self.n += 1
        return ins

    def wait(self):
        self.eng.wait_ge(self.sem, self.n)


def build(nc, a, out):
    with ExitStack() as ctx:
        def sb(name, *shape):
            return ctx.enter_context(nc.sbuf_tensor(name, [P, *shape], F32))

        H = sb("H", KT, T)
        Y = sb("Y", KT, T)
        U = sb("U", 15360)
        RAW = sb("RAW", T + 4)
        W = sb("W", 2, KT * P)
        CST = sb("CST", N_CST)
        MOD = sb("MOD", 24, 2)
        GAIN = sb("GAIN", KT, 2)
        NG = sb("NG", KT)
        CC = sb("CC", KT, 2)
        ADAB = sb("ADAB", 24)
        RKC = sb("RKC", N_RKC)
        RKU = sb("RKU", N_RKU)
        MU = sb("MU", 3, 5)
        RTU = sb("RTU", N_RTU)
        GDU = sb("GDU", 2 * N_GDU)
        GS = sb("GS", NCH, 4, 2, N_GS)
        GSU = sb("GSU", NCH, 2, 2, N_GS)
        GP = sb("GP", 2, 8)
        ST = sb("ST", 3, 2 * NCH)
        FG = sb("FG", KT)
        SL = sb("SL", 8 * 512)
        XS = sb("XS", 4, P)
        YS = sb("YS", 4, P)
        QS = sb("QS", 4, P)
        SLOT = sb("SLOT", 1024)
        KTOK = sb("KTOK", 512)
        STATE = sb("STATE", 512)
        SC = sb("SC", 2, 2, N_GS)
        PS = [ctx.enter_context(nc.psum_tensor(f"PS{b}", [P, 512], F32)) for b in range(8)]
        x_next = nc.dram_tensor("x_next", (KT, P, T), F32, kind="Internal").ap()
        v_first = nc.dram_tensor("v_first", (2, P, T), F32, kind="Internal").ap()

        def cst(at, n=P):
            return CST[:, at:at + n]

        IDENT, ONES, BLK = cst(C_IDENT), cst(C_ONES), cst(C_BLK)
        YT = [Y[:, t, :] for t in range(KT)]

        def pieces(ps=0):
            return [(PS[ps + n], t0, m) for n, (t0, m) in enumerate(PIECES)]

        def chunked(tile):
            return tile.rearrange("p (c t) -> p c t", t=CH)

        def load_weights(sp, s, tile_of, n, layer):
            for j in range(n):
                if j >= 2:
                    sp.wait_ge(s["projected"], 3 * (j - 1))
                sp.dma_start(W[:, j % 2, :], a["w_t"][layer, bass.ds(tile_of + j, 1)].rearrange("a p n -> p (a n)")
                             ).then_inc(s[f"w_loaded{j % 2}"], 16)
            for q in range(2):
                sp.wait_ge(s[f"w_loaded{q}"], 16 * ((n - 1 - q) // 2 + 1))

        def project(pe, s, j):
            pe.wait_ge(s[f"w_loaded{j % 2}"], 16 * (j // 2 + 1))
            for n, (bank, t0, m) in enumerate(pieces()):
                if j:
                    pe.wait_ge(s["taken"], 3 * (j - 1) + n + 1)
                for k in range(KT):
                    mm = nc.tensor.matmul(bank[:, 0:m], W[:, j % 2, k * P:(k + 1) * P], H[:, k, t0:t0 + m],
                                          start=(k == 0), stop=(k == KT - 1))
                mm.then_inc(s["projected"], 1)

        def rsqrt_sum(act, s, link, bank, m, dst, scale, eps, after):
            link(nc.scalar.activation(dst, bank[:, 0:m], ACT.Ln, scale=scale, bias=eps))
            link.wait()
            nc.scalar.activation(dst, dst, ACT.Exp, scale=-0.5, bias=after)

        def column_sums(pe, tile, weights, ps=0):
            for bank, t0, m in pieces(ps):
                mm = nc.tensor.matmul(bank[:, 0:m], weights, tile[:, t0:t0 + m], start=True, stop=True)
            return mm

        EPSC = sb("EPSC", 4)
        HALF_LN = -0.5 * math.log(P)
        with Stage(nc, "loaded") as (block, s):
            @block.sync
            def _(sp):
                sp.dma_start(CST[:, :], a["consts"]).then_inc(s["loaded"], 16)
                sp.dma_start(CC[:, :, :], a["cc"]).then_inc(s["loaded"], 16)
                sp.dma_start(FG[:, :], a["final_g"]).then_inc(s["loaded"], 16)
                sp.dma_start(H[:, :, :], a["xT"].rearrange("k p t -> p k t")).then_inc(s["loaded"], 16)
                sp.wait_ge(s["loaded"], 64)

            @block.gpsimd
            def _(pool):
                nc.gpsimd.memset(RAW[:, :], 0.0)
                nc.gpsimd.memset(EPSC[:, 0:1], EPS)
                nc.gpsimd.memset(EPSC[:, 1:2], LN_EPS)
                nc.gpsimd.memset(EPSC[:, 2:3], HALF_LN)
                nc.gpsimd.memset(EPSC[:, 3:4], 1.0)

        with Stage(nc, "ready") as (block, s):
            @block.scalar
            def _(act):
                nc.scalar.activation(CC[:, :, :], CC[:, :, :], ACT.Silu)

        EPS_C, LNEPS_C, HALFLN_C, ONE_C = (EPSC[:, q:q + 1] for q in range(4))

        def modulation(layer):
            AW = U[:, 0:2 * KT * 384].rearrange("p (b k n) -> p b k n", b=2, k=KT)
            with Stage(nc, "w_loaded0 w_loaded1 small_loaded multiplied order") as (block, s):
                @block.sync
                def _(sp):
                    sp.dma_start(ADAB[:, :], a["ada_b"][layer]).then_inc(s["small_loaded"], 16)
                    sp.dma_start(NG[:, :], a["norm_g"][layer]).then_inc(s["small_loaded"], 16)
                    sp.dma_start(RKC[:, :], a["rkc"][layer]).then_inc(s["small_loaded"], 16)
                    sp.dma_start(GP[:, :, :], a["gda"][layer]).then_inc(s["small_loaded"], 16)
                    for g in range(8):
                        if g >= 2:
                            sp.wait_ge(s["multiplied"], g - 1)
                        sp.dma_start(AW[:, g % 2], a["ada_w"][layer, g]).then_inc(s[f"w_loaded{g % 2}"], 16)

                @block.tensor
                def _(pe):
                    for g in range(8):
                        pe.wait_ge(s[f"w_loaded{g % 2}"], 16 * (g // 2 + 1))
                        for n in range(3):
                            for k in range(KT):
                                mm = nc.tensor.matmul(PS[0][:, 2 * (3 * g + n):2 * (3 * g + n) + 2],
                                                      AW[:, g % 2, k, n * P:(n + 1) * P], CC[:, k, :],
                                                      start=(k == 0), stop=(k == KT - 1))
                        mm.then_inc(s["multiplied"], 1)

                @block.vector
                def _(dve):
                    dve.wait_ge(s["small_loaded"], 64)
                    dve.wait_ge(s["multiplied"], 8)
                    link = Link(dve, s["order"])
                    link(nc.vector.tensor_tensor(MOD[:, :, :], PS[0][:, 0:48].rearrange("p (n v) -> p n v", v=2),
                                                 ADAB[:, :, None].to_broadcast([P, 24, 2]), ALU.add))
                    link.wait()
                    link(nc.vector.tensor_scalar(GAIN[:, :, :], MOD[:, 8:16, :], 1.0, None, ALU.add))
                    link.wait()
                    nc.vector.tensor_tensor(GAIN[:, :, :], GAIN[:, :, :], NG[:, :, None].to_broadcast([P, KT, 2]), ALU.mult)

        RSTD = U[:, 0:T]
        SQ = [U[:, T * (1 + q):T * (2 + q)] for q in range(2)]

        def mean_square(block, s):
            @block.scalar
            def _(act):
                link = Link(act, s["act_order"])
                for k in range(KT):
                    if k >= 2:
                        act.wait_ge(s["summed"], k - 1)
                    nc.scalar.activation(SQ[k % 2], H[:, k, :], ACT.Square).then_inc(s["squared"], 1)
                act.wait_ge(s["summed"], KT)
                for bank, t0, m in pieces():
                    link(nc.scalar.activation(RSTD[:, t0:t0 + m], bank[:, 0:m], ACT.Ln, scale=1.0 / D, bias=EPS_C))
                link.wait()
                nc.scalar.activation(RSTD, RSTD, ACT.Exp, scale=-0.5).then_inc(s["rstd_ready"], 1)

            @block.tensor
            def _(pe):
                for k in range(KT):
                    pe.wait_ge(s["squared"], k + 1)
                    for bank, t0, m in pieces():
                        mm = nc.tensor.matmul(bank[:, 0:m], ONES, SQ[k % 2][:, t0:t0 + m], start=(k == 0), stop=(k == KT - 1))
                    mm.then_inc(s["summed"], 1)

        def normalise():
            with Stage(nc, "squared summed rstd_ready act_order order") as (block, s):
                mean_square(block, s)

                @block.vector
                def _(dve):
                    dve.wait_ge(s["rstd_ready"], 1)
                    link = Link(dve, s["order"])
                    for k in range(KT):
                        link(nc.vector.tensor_tensor(H[:, k, :], H[:, k, :], RSTD, ALU.mult))
                    for k in range(KT):
                        dve.wait_ge(s["order"], k + 1)
                        for v, (t0, t1) in enumerate(((CTX, T), (0, CTX))):
                            nc.vector.tensor_scalar(H[:, k, t0:t1], H[:, k, t0:t1], GAIN[:, k, v:v + 1], MOD[:, k, v:v + 1],
                                                    ALU.mult, ALU.add)

        def mix(dve, link, dst, t, done):
            raw_c, raw_l = RAW[:, 1:1 + CTX], RAW[:, CTX + 3:CTX + 3 + SEQ]

            def coef(q):
                return MU[:, t, q:q + 1]

            def add(o, i, q):
                link.wait()
                link(nc.vector.scalar_tensor_tensor(o, i, coef(q), o, ALU.mult, ALU.add))

            link(nc.vector.tensor_scalar(dst[:, 0:CTX], raw_c, coef(0), None, ALU.mult))
            link(nc.vector.tensor_scalar(dst[:, CTX:T], raw_l, coef(0), None, ALU.mult))
            for q, back in ((1, True), (2, False), (3, True), (4, False)):
                if back:
                    add(dst[:, 1:CTX], raw_c[:, 0:CTX - 1], q)
                else:
                    add(dst[:, 0:CTX - 1], raw_c[:, 1:CTX], q)
            lat, src = dst[:, CTX:T].rearrange("p (r w) -> p r w", w=GRID), raw_l.rearrange("p (r w) -> p r w", w=GRID)
            add(lat[:, :, 1:GRID], src[:, :, 0:GRID - 1], 1)
            add(lat[:, :, 0:GRID - 1], src[:, :, 1:GRID], 2)
            add(dst[:, CTX + GRID:T], raw_l[:, 0:SEQ - GRID], 3)
            link.wait()
            nc.vector.scalar_tensor_tensor(dst[:, CTX:T - GRID], raw_l[:, GRID:SEQ], coef(4), dst[:, CTX:T - GRID],
                                           ALU.mult, ALU.add).then_inc(done, 1)

        def mu_columns(dve, link, src, n):
            link(nc.vector.tensor_scalar(MU[:, 0:n, 0], src, -1.0, 1.0, ALU.mult, ALU.add))
            for t in range(n):
                link(nc.vector.tensor_scalar(MU[:, t, 1:5], cst(C_TYPE, 4), src[:, t:t + 1], None, ALU.mult))
            link.wait()

        def raw_of(t0, m):
            return RAW[:, 1:1 + CTX] if t0 < CTX else RAW[:, t0 + 3:t0 + 3 + m]

        VT = [U[:, 0:T], U[:, T:2 * T]]
        WA = U[:, 2 * T:3 * T]
        VTOK = U[:, 3 * T:4 * T].rearrange("p (c n) -> p c n", c=NCH)
        PKG = U[:, 4 * T:12 * T].rearrange("p (d c f t) -> p d c f t", d=2, c=NCH, f=4)

        def rwkv_common(layer):
            with Stage(nc, "w_loaded0 w_loaded1 projected taken mixed act_order order stored vf_loaded "
                           "v1_done v1_taken v2_done v2_sig") as (block, s):
                dsts = [VT[0], VT[1], WA]

                @block.sync
                def _(sp):
                    load_weights(sp, s, W_RK_COMMON, 3, layer)
                    sp.wait_ge(s["mixed"], 3)
                    if layer == 0:
                        for q in range(2):
                            sp.dma_start(v_first[q], VT[q]).then_inc(s["stored"], 16)
                        sp.wait_ge(s["stored"], 32)
                    else:
                        for q in range(2):
                            sp.dma_start(YT[q], v_first[q]).then_inc(s["vf_loaded"], 16)

                @block.tensor
                def _(pe):
                    for j in range(3):
                        project(pe, s, j)
                    if layer:
                        pe.wait_ge(s["mixed"], 2)
                        for bank, t0, m in pieces(3):
                            for q in range(2):
                                mm = nc.tensor.matmul(bank[0:32, 0:m], RKC[:, RKC_V1 + 32 * q:RKC_V1 + 32 * (q + 1)],
                                                      VT[q][:, t0:t0 + m], start=(q == 0), stop=(q == 1))
                        mm.then_inc(s["v1_done"], 1)
                        pe.wait_ge(s["v1_taken"], 1)
                        for q in range(2):
                            if q:
                                pe.wait_ge(s["v2_sig"], 1)
                            for bank, t0, m in pieces(3):
                                mm = nc.tensor.matmul(bank[:, 0:m], RKC[0:32, RKC_V2 + P * q:RKC_V2 + P * (q + 1)],
                                                      YT[2][0:32, t0:t0 + m], start=True, stop=True)
                            mm.then_inc(s["v2_done"], 1)

                @block.scalar
                def _(act):
                    for j in range(3):
                        for n, (bank, t0, m) in enumerate(pieces()):
                            act.wait_ge(s["projected"], 3 * j + n + 1)
                            if j and n == 0:
                                act.wait_ge(s["mixed"], j)
                            nc.scalar.copy(raw_of(t0, m), bank[:, 0:m]).then_inc(s["taken"], 1)
                    act.wait_ge(s["mixed"], 3)
                    nc.scalar.activation(WA[0:64], WA[0:64], ACT.Tanh)
                    if layer:
                        act.wait_ge(s["v1_done"], 1)
                        for bank, t0, m in pieces(3):
                            ins = nc.scalar.copy(YT[2][0:32, t0:t0 + m], bank[0:32, 0:m])
                        ins.then_inc(s["v1_taken"], 1)
                        for q in range(2):
                            act.wait_ge(s["v2_done"], q + 1)
                            for bank, t0, m in pieces(3):
                                ins = nc.scalar.activation(YT[4 + q][:, t0:t0 + m], bank[:, 0:m], ACT.Sigmoid,
                                                           bias=RKC[:, RKC_V0 + q:RKC_V0 + q + 1])
                            ins.then_inc(s["v2_sig"], 1)

                @block.vector
                def _(dve):
                    link = Link(dve, s["order"])
                    mu_columns(dve, link, RKC[:, RKC_MU:RKC_MU + 3], 3)
                    for j in range(3):
                        dve.wait_ge(s["taken"], 3 * (j + 1))
                        mix(dve, link, dsts[j], j, s["mixed"])
                    if layer:
                        dve.wait_ge(s["vf_loaded"], 32)
                        for q in range(2):
                            link(nc.vector.tensor_tensor(YT[q], YT[q], VT[q], ALU.subtract))
                            dve.wait_ge(s["v2_sig"], q + 1)
                            link.wait()
                            link(nc.vector.tensor_tensor(YT[q], YT[q], YT[4 + q], ALU.mult))
                            link.wait()
                            link(nc.vector.tensor_tensor(VT[q], YT[q], VT[q], ALU.add))

        def rwkv_project(layer, p):
            with Stage(nc, "w_loaded0 w_loaded1 projected taken mixed order param_loaded v_copied "
                           "kk_squared kk_summed kk_ln kk_rstd turned") as (block, s):
                @block.sync
                def _(sp):
                    sp.dma_start(RKU[:, :], a["rku"][layer, bass.ds(p, 1)].rearrange("a q n -> q (a n)")
                                 ).then_inc(s["param_loaded"], 16)
                    load_weights(sp, s, W_RK + 3 * p, 3, layer)
                    sp.wait_ge(s["param_loaded"], 16)

                @block.tensor
                def _(pe):
                    for j in range(3):
                        project(pe, s, j)
                    pe.wait_ge(s["v_copied"], 1)
                    for c in range(NCH):
                        bank, col = (PS[3], c * P) if c < 2 else (PS[4 + (c - 2) // 4], (c - 2) % 4 * P)
                        tr = nc.tensor.transpose(bank[:, col:col + P], PT[:, c * P:(c + 1) * P], IDENT)
                    tr.then_inc(s["turned"], 1)
                    pe.wait_ge(s["kk_squared"], 1)
                    pe.wait_ge(s["taken"], 9)
                    column_sums(pe, L, BLK).then_inc(s["kk_summed"], 1)

                @block.scalar
                def _(act):
                    for j in range(2):
                        for n, (bank, t0, m) in enumerate(pieces()):
                            act.wait_ge(s["projected"], 3 * j + n + 1)
                            if j and n == 0:
                                act.wait_ge(s["mixed"], j)
                            nc.scalar.copy(raw_of(t0, m), bank[:, 0:m]).then_inc(s["taken"], 1)
                    for n, (bank, t0, m) in enumerate(pieces()):
                        act.wait_ge(s["projected"], 7 + n)
                        nc.scalar.activation(Y[:, bass.ds(p, 1), t0:t0 + m], bank[:, None, 0:m], ACT.Silu).then_inc(s["taken"], 1)
                    act.wait_ge(s["turned"], 1)
                    for bank, t0, m in pieces(3):
                        nc.scalar.copy(VTOK[:, t0 // P:(t0 + m) // P, :], bank[:, 0:m].rearrange("p (c n) -> p c n", n=P))
                    act.wait_ge(s["kk_summed"], 1)
                    for bank, t0, m in pieces():
                        ins = nc.scalar.activation(L[:, t0:t0 + m], bank[:, 0:m], ACT.Ln, bias=EPS_C)
                    ins.then_inc(s["kk_ln"], 1)
                    act.wait_ge(s["kk_ln"], 1)
                    nc.scalar.activation(L, L, ACT.Exp, scale=-0.5).then_inc(s["kk_rstd"], 1)

                @block.vector
                def _(dve):
                    link = Link(dve, s["order"])
                    nc.vector.tensor_copy(PT[:, None, :], U[:, 0:2 * T].rearrange("p (q t) -> p q t", q=2)[:, bass.ds(p, 1), :]
                                          ).then_inc(s["v_copied"], 1)
                    dve.wait_ge(s["param_loaded"], 16)
                    mu_columns(dve, link, RKU[:, RKU_MU:RKU_MU + 2], 2)
                    for j, dst in enumerate((R, K)):
                        dve.wait_ge(s["taken"], 3 * (j + 1))
                        mix(dve, link, dst, j, s["mixed"])
                    dve.wait_ge(s["mixed"], 2)
                    link(nc.vector.tensor_scalar(KK, K, RKU[:, RKU_KK:RKU_KK + 1], None, ALU.mult))
                    link.wait()
                    nc.vector.tensor_tensor(L, KK, KK, ALU.mult).then_inc(s["kk_squared"], 1)
                    dve.wait_ge(s["kk_rstd"], 1)
                    nc.vector.tensor_tensor(KK, KK, L, ALU.mult)

        R, K, KK, L, PT, IC = YT[2], YT[3], YT[4], YT[5], YT[6], YT[7]
        EC = sb("EC", 2, NCH + 1)

        def rwkv_packages(p, d):
            with Stage(nc, "lora_done sigmoids log_ready exp_ready used order bonus_ready bonus_summed") as (block, s):
                @block.tensor
                def _(pe):
                    for row, ps in ((0, 0), (64, 3)):
                        for bank, t0, m in pieces(ps):
                            mm = nc.tensor.matmul(bank[:, 0:m], RKU[row:row + 64, d * P:(d + 1) * P],
                                                  WA[row:row + 64, t0:t0 + m], start=True, stop=True)
                    mm.then_inc(s["lora_done"], 1)
                    if d:
                        pe.wait_ge(s["sigmoids"], 1)
                        pe.wait_ge(s["bonus_ready"], 1)
                        column_sums(pe, RAW, BLK).then_inc(s["bonus_summed"], 1)

                @block.scalar
                def _(act):
                    act.wait_ge(s["lora_done"], 1)
                    for bank, t0, m in pieces(0):
                        nc.scalar.activation(L[:, t0:t0 + m], bank[:, 0:m], ACT.Sigmoid, bias=RKU[:, RKU_W0 + d:RKU_W0 + d + 1])
                    for bank, t0, m in pieces(3):
                        ins = nc.scalar.activation(IC[:, t0:t0 + m], bank[:, 0:m], ACT.Sigmoid,
                                                   bias=RKU[:, RKU_A0 + d:RKU_A0 + d + 1])
                    ins.then_inc(s["sigmoids"], 1)
                    excl = (RAW[:, 0:T], 1.0) if d == 0 else (PT, -1.0)
                    incl = PT if d == 0 else L
                    for q, (src, sign) in enumerate((excl, (incl, 1.0), (incl, -1.0))):
                        act.wait_ge(s["log_ready"], 1)
                        if q:
                            act.wait_ge(s["used"], q)
                        nc.scalar.activation(RAW[:, 0:T], src, ACT.Exp, scale=sign).then_inc(s["exp_ready"], 1)
                    nc.scalar.activation(EC[:, d, 0:NCH], EC[:, d, 0:NCH], ACT.Exp)

                @block.vector
                def _(dve):
                    link = Link(dve, s["order"])
                    ic_f = PKG[:, 1, :, 3, :]
                    dve.wait_ge(s["sigmoids"], 1)
                    link(nc.vector.tensor_scalar(L, L, NEG_SQRT_E, None, ALU.mult))
                    link(nc.vector.memset(EC[:, d, NCH:NCH + 1], 1.0))
                    link.wait()
                    for c in range(NCH):
                        link(nc.vector.tensor_tensor_scan(PT[:, c * P:(c + 1) * P], ONES, L[:, c * P:(c + 1) * P], 0.0,
                                                          ALU.mult, ALU.add))
                    link.wait()
                    link(nc.vector.tensor_scalar(EC[:, d, 0:NCH], chunked(PT)[:, :, P - 1], 0.5, None, ALU.mult))
                    link.wait()
                    link(nc.vector.tensor_tensor(chunked(PT), chunked(PT), EC[:, d, 0:NCH, None].to_broadcast([P, NCH, P]),
                                                 ALU.subtract))
                    link.wait()
                    if d == 0:
                        link(nc.vector.tensor_copy(ic_f, chunked(IC)))
                        nc.vector.tensor_tensor(RAW[:, 0:T], PT, L, ALU.subtract).then_inc(s["log_ready"], 1)
                    else:
                        link(nc.vector.tensor_tensor(chunked(RAW[:, 0:T]), ic_f, chunked(IC), ALU.add))
                        link.wait()
                        link(nc.vector.tensor_scalar(RAW[:, 0:T], RAW[:, 0:T], -2.0, RKU[:, RKU_KA:RKU_KA + 1], ALU.add, ALU.mult))
                        link.wait()
                        link(nc.vector.scalar_tensor_tensor(RAW[:, 0:T], RAW[:, 0:T], 2.0, K, ALU.add, ALU.mult))
                        link.wait()
                        nc.vector.scalar_tensor_tensor(RAW[:, 0:T], R, RKU[:, RKU_RK:RKU_RK + 1], RAW[:, 0:T],
                                                       ALU.mult, ALU.mult).then_inc(s["bonus_ready"], 1)
                        dve.wait_ge(s["bonus_summed"], 1)
                        for bank, t0, m in pieces():
                            vp = U[:, 0:2 * T].rearrange("p (q t) -> p q t", q=2)[:, bass.ds(p, 1), t0:t0 + m]
                            link(nc.vector.tensor_tensor(vp, vp, bank[:, None, 0:m], ALU.mult))
                        nc.vector.tensor_tensor(L, L, PT, ALU.subtract).then_inc(s["log_ready"], 1)
                    dve.wait_ge(s["exp_ready"], 1)
                    nc.vector.tensor_tensor(PKG[:, d, :, 0, :], chunked(KK), chunked(RAW[:, 0:T]), ALU.mult).then_inc(s["used"], 1)
                    dve.wait_ge(s["exp_ready"], 2)
                    nc.vector.tensor_tensor(PKG[:, d, :, 1, :], chunked(R), chunked(RAW[:, 0:T]), ALU.mult).then_inc(s["used"], 1)
                    dve.wait_ge(s["exp_ready"], 3)
                    link(nc.vector.tensor_scalar(L, IC, -1.0, RKU[:, RKU_KA:RKU_KA + 1], ALU.add, ALU.mult))
                    link(nc.vector.tensor_tensor(IC, IC, KK, ALU.mult))
                    link.wait()
                    link(nc.vector.scalar_tensor_tensor(L, L, 1.0, K, ALU.add, ALU.mult))
                    link.wait()
                    nc.vector.tensor_tensor(PKG[:, d, :, 2, :], chunked(L), chunked(RAW[:, 0:T]), ALU.mult)
                    nc.vector.tensor_tensor(PKG[:, d, :, 3, :], chunked(IC), chunked(RAW[:, 0:T]), ALU.mult)

        def lvl(level, d):
            at = C_LVL + (level * 2 + d) * P
            return CST[:, at:at + P]

        def lvl2(level):
            at = C_LVL + level * 2 * P
            return CST[:, at:at + 2 * P].rearrange("p (d n) -> p d n", d=2)[:, :, None, :].to_broadcast([P, 2, 2, P])

        def by_dir(tile):
            return tile.rearrange("p (d h) n -> p d h n", d=2)

        SOLVER = "ut_ready lu_done q_ready xy_done x_taken y_taken "

        def solve_tensor(pe, s, ut):
            for lv in range(LEVELS):
                if lv:
                    pe.wait_ge(s["x_taken"], lv)
                for m in range(4):
                    mm = nc.tensor.matmul(PS[4][:, m * P:(m + 1) * P], ut(m), IDENT if lv == 0 else XS[:, m, :],
                                          start=True, stop=True)
                mm.then_inc(s["lu_done"], 1)
                if lv == 0:
                    continue
                pe.wait_ge(s["q_ready"], lv)
                pe.wait_ge(s["y_taken"], lv)
                if lv < LEVELS - 1:
                    for m in range(4):
                        mm = nc.tensor.matmul(PS[5][:, m * P:(m + 1) * P], YS[:, m, :], QS[:, m, :], start=True, stop=True)
                    mm.then_inc(s["xy_done"], 1)
                for m in range(4):
                    mm = nc.tensor.matmul(PS[6][:, m * P:(m + 1) * P], QS[:, m, :], YS[:, m, :], start=True, stop=True)
                mm.then_inc(s["xy_done"], 1)

        def solve_vector(dve, s, ut4):
            for lv in range(LEVELS):
                dve.wait_ge(s["lu_done"], lv + 1)
                if lv == 0:
                    nc.vector.tensor_tensor(by_dir(XS[:, :, :]), PS[4][:, :].rearrange("p (d h n) -> p d h n", d=2, h=2), lvl2(0),
                                            ALU.mult).then_inc(s["x_taken"], 1)
                    for d in range(2):
                        ins = nc.vector.tensor_tensor(YS[:, 2 * d:2 * d + 2, :], ut4(d),
                                                      lvl(0, 1 - d)[:, None, :].to_broadcast([P, 2, P]), ALU.mult)
                    ins.then_inc(s["y_taken"], 1)
                    continue
                nc.vector.tensor_tensor(by_dir(QS[:, :, :]), PS[4][:, :].rearrange("p (d h n) -> p d h n", d=2, h=2), lvl2(lv),
                                        ALU.mult).then_inc(s["q_ready"], 1)

        def solve_scalar(act, s):
            for lv in range(1, LEVELS):
                last = lv == LEVELS - 1
                if not last:
                    act.wait_ge(s["xy_done"], 2 * lv - 1)
                    nc.scalar.copy(XS[:, :, :], PS[5][:, :].rearrange("p (m n) -> p m n", m=4)).then_inc(s["x_taken"], 1)
                act.wait_ge(s["xy_done"], 2 * lv if not last else 2 * lv - 1)
                nc.scalar.copy(YS[:, :, :], PS[6][:, :].rearrange("p (m n) -> p m n", m=4)).then_inc(s["y_taken"], 1)

        SCO = SL[:, 0:2048].rearrange("p (m f n) -> p m f n", m=4, f=4)
        RS = SLOT[:, :].rearrange("p (d f t) -> p d f t", d=2, f=4)
        R1S = SL[:, 2048:2304].rearrange("p (m n) -> p m n", m=4)
        NZ = SL[:, 2304:2560].rearrange("p (m n) -> p m n", m=4)
        VS = SL[:, 2560:2816].rearrange("p (d n) -> p d n", d=2)
        SUM = SL[:, 2816:2944].rearrange("p (d n) -> p d n", d=2)
        ECS = SL[:, 2944:2948].rearrange("p (d q) -> p d q", d=2)
        TK = KTOK[:, :].rearrange("p (d f n) -> p d f n", d=2, f=2)
        RST = STATE[:, 0:128].rearrange("p (d n) -> p d n", d=2)

        def at(c):
            return slice(c, c + 1) if isinstance(c, int) else bass.ds(c, 1)

        def rwkv_init():
            with Stage(nc, "order") as (block, s):
                @block.vector
                def _(dve):
                    link = Link(dve, s["order"])
                    link(nc.vector.memset(SCO, 0.0))
                    link(nc.vector.memset(RST, 0.0))
                    link.wait()
                    nc.vector.tensor_copy(SCO[:, :, 2, :], IDENT[:, None, :].to_broadcast([P, 4, P]))

        R1_BANK = (7, 3)

        def rwkv_step(cf, cb, nf, nb):
            with Stage(nc, SOLVER + "slots_ready v_ready scored masked turned turn_taken r1_done r1_taken z_done z_taken "
                           "o_done kv_done sum order") as (block, s):
                @block.scalar
                def _(act):
                    for d, c in enumerate((cf, cb)):
                        nc.scalar.copy(RS[:, d:d + 1], PKG[:, d, at(c)]).then_inc(s["slots_ready"], 1)
                    act.wait_ge(s["turned"], 1)
                    nc.scalar.copy(TK, PS[7][:, :].rearrange("p (d f n) -> p d f n", d=2, f=2)).then_inc(s["turn_taken"], 1)
                    solve_scalar(act, s)
                    act.wait_ge(s["r1_done"], 1)
                    for h in range(2):
                        nc.scalar.copy(R1S.rearrange("p (d h) n -> p h d n", h=2)[:, h],
                                       PS[R1_BANK[h]][:, 0:P].rearrange("p (d n) -> p d n", d=2)).then_inc(s["r1_taken"], 1)
                    act.wait_ge(s["z_done"], 1)
                    nc.scalar.activation(NZ, PS[0][:, 0:256].rearrange("p (m n) -> p m n", m=4), ACT.Copy, scale=-1.0
                                         ).then_inc(s["z_taken"], 1)
                    act.wait_ge(s["o_done"], 1)
                    for d, c in enumerate((cf, cb)):
                        for h in range(2):
                            nc.scalar.copy(PKG[:, d, at(c), 0, 64 * h:64 * h + 64], PS[1 + h][:, None, 64 * d:64 * d + 64])

                @block.tensor
                def _(pe):
                    for d in range(2):
                        pe.wait_ge(s["slots_ready"], d + 1)
                        for h in range(2):
                            rows = slice(64 * h, 64 * h + 64)
                            for f in range(2):
                                mm = nc.tensor.matmul(PS[2 * d + h][:, 256 * f:256 * f + 256], RS[rows, d, 2 + f, :],
                                                      RS[rows, d, 0:2, :], start=True, stop=True)
                            mm.then_inc(s["scored"], 1)
                    for d in range(2):
                        for f in range(2):
                            mm = nc.tensor.transpose(PS[7][:, (2 * d + f) * P:(2 * d + f + 1) * P], RS[:, d, 2 + f, :], IDENT)
                    mm.then_inc(s["turned"], 1)
                    pe.wait_ge(s["masked"], 4)
                    solve_tensor(pe, s, lambda m: SCO[:, m, 2, :])
                    pe.wait_ge(s["turn_taken"], 1)
                    pe.wait_ge(s["v_ready"], 2)
                    heads = [(m, m // 2, slice(64 * (m % 2), 64 * (m % 2) + 64)) for m in range(4)]
                    for m, d, rows in heads:
                        o = PS[R1_BANK[m % 2]][:, 64 * d:64 * d + 64]
                        nc.tensor.matmul(o, RS[rows, d, 0, :], RST[rows, d, :], start=True, stop=False)
                        mm = nc.tensor.matmul(o, SCO[:, m, 0, :], VS[:, d, rows], start=False, stop=True)
                    mm.then_inc(s["r1_done"], 1)
                    pe.wait_ge(s["r1_taken"], 2)
                    pe.wait_ge(s["y_taken"], LEVELS)
                    for m, d, rows in heads:
                        mm = nc.tensor.matmul(PS[0][:, 64 * m:64 * m + 64], YS[:, m, :], R1S[:, m, :], start=True, stop=True)
                    mm.then_inc(s["z_done"], 1)
                    pe.wait_ge(s["z_taken"], 1)
                    for m, d, rows in heads:
                        o = PS[1 + m % 2][:, 64 * d:64 * d + 64]
                        nc.tensor.matmul(o, RS[rows, d, 1, :], RST[rows, d, :], start=True, stop=False)
                        nc.tensor.matmul(o, SCO[:, m, 1, :], VS[:, d, rows], start=False, stop=False)
                        mm = nc.tensor.matmul(o, SCO[:, m, 3, :], NZ[:, m, :], start=False, stop=True)
                    mm.then_inc(s["o_done"], 1)
                    for m, d, rows in heads:
                        o = PS[0][rows, 64 * d:64 * d + 64]
                        nc.tensor.matmul(o, TK[:, d, 0, rows], VS[:, d, rows], start=True, stop=False)
                        mm = nc.tensor.matmul(o, TK[:, d, 1, rows], NZ[:, m, :], start=False, stop=True)
                    mm.then_inc(s["kv_done"], 1)

                @block.vector
                def _(dve):
                    link = Link(dve, s["order"])
                    for d, (c, n) in enumerate(((cf, nf), (cb, nb))):
                        nc.vector.tensor_copy(VS[:, d:d + 1, :], VTOK[:, at(c), :]).then_inc(s["v_ready"], 1)
                        link(nc.vector.tensor_copy(ECS[:, d, 0:1], EC[:, d, at(c)]))
                        link(nc.vector.tensor_copy(ECS[:, d, 1:2], EC[:, d, at(n)]))
                    for m in range(4):
                        d = m // 2
                        dve.wait_ge(s["scored"], m + 1)
                        mask = CST[:, C_SI + d * 256:C_SI + (d + 1) * 256].bitcast(I32)[:, None, :].to_broadcast([P, 2, 256])
                        nc.vector.copy_predicated(SCO[:, m].rearrange("p (q g) n -> p q (g n)", q=2), mask,
                                                  PS[m][:, :].rearrange("p (q n) -> p q n", q=2)).then_inc(s["masked"], 1)
                    dve.wait_ge(s["masked"], 4)
                    solve_vector(dve, s, lambda d: SCO[:, 2 * d:2 * d + 2, 2, :])
                    dve.wait_ge(s["kv_done"], 1)
                    link(nc.vector.tensor_tensor(SUM, RST, PS[0][:, 0:P].rearrange("p (d n) -> p d n", d=2), ALU.add))
                    link.wait()
                    for d in range(2):
                        nc.vector.tensor_scalar(RST[:, d, :], SUM[:, d, :], ECS[:, d, 0:1], ECS[:, d, 1:2], ALU.mult, ALU.mult)

        def scan(step, init):
            init()
            step(0, 1, 1, 0)
            step(1, 0, NC_CTX, NCH - 1)
            with nc.Fori(0, NCH - NC_CTX) as i:
                step(NC_CTX + i, NCH - 1 - i, NC_CTX + 1 + i, NCH - 2 - i)

        def normalise_heads(block, s, o_f, o_b, o, sq, heads, centred, eps):
            width = o.shape[3]

            @block.vector
            def _(dve):
                link = Link(dve, s["order"])
                n = NCH * heads
                mean, var, scale = (ST[:, q, 0:n].rearrange("p (c h) -> p c h", h=heads) for q in range(3))

                def wide(st):
                    return st[:, :, :, None].to_broadcast([P, NCH, heads, width])

                if o_b is not None:
                    link(nc.vector.tensor_tensor(o, o_f, o_b, ALU.add))
                    link.wait()
                if centred:
                    link(nc.vector.tensor_reduce(mean, o, AX, ALU.add))
                    link.wait()
                    link(nc.vector.tensor_scalar(mean, mean, 1.0 / width, None, ALU.mult))
                    link.wait()
                    link(nc.vector.tensor_tensor(o, o, wide(mean), ALU.subtract))
                    link.wait()
                link(nc.vector.tensor_tensor(sq, o, o, ALU.mult))
                link.wait()
                nc.vector.tensor_reduce(var, sq, AX, ALU.add).then_inc(s["var_ready"], 1)
                dve.wait_ge(s["rstd_ready"], 2)
                nc.vector.tensor_tensor(o, o, wide(scale), ALU.mult).then_inc(s["o_ready"], 1)

            def rstd(act):
                n = NCH * heads
                act.wait_ge(s["var_ready"], 1)
                nc.scalar.activation(ST[:, 2, 0:n], ST[:, 1, 0:n], ACT.Ln, scale=1.0 / width, bias=eps).then_inc(s["rstd_ready"], 1)
                act.wait_ge(s["rstd_ready"], 1)
                nc.scalar.activation(ST[:, 2, 0:n], ST[:, 2, 0:n], ACT.Exp, scale=-0.5).then_inc(s["rstd_ready"], 1)

            return rstd

        def turn_outputs(pe, s, o, turn):
            for c in range(NCH):
                bank, col = (PS[0], c * P) if c < 2 else (PS[1 + (c - 2) // 4], (c - 2) % 4 * P)
                tr = nc.tensor.transpose(bank[:, col:col + P], o[:, c, :], IDENT)
            tr.then_inc(s["turned"], 1)

        def rwkv_post(p):
            o = PKG[:, 0, :, 1, :]
            with Stage(nc, "var_ready rstd_ready o_ready turned order out_order copied") as (block, s):
                heads = lambda x: x.rearrange("p c (h n) -> p c h n", h=2)
                OC = chunked(YT[2])
                rstd = normalise_heads(block, s, heads(PKG[:, 0, :, 0, :]), heads(PKG[:, 1, :, 0, :]), heads(OC),
                                       heads(chunked(YT[3])), 2, True, LNEPS_C)

                @block.scalar
                def _(act):
                    rstd(act)

                @block.tensor
                def _(pe):
                    pe.wait_ge(s["o_ready"], 1)
                    turn_outputs(pe, s, OC, None)
            with Stage(nc, "order") as (block, s):
                @block.vector
                def _(dve):
                    link = Link(dve, s["order"])
                    for bank, t0, m in pieces():
                        bonus = U[:, 0:2 * T].rearrange("p (q t) -> p q t", q=2)[:, bass.ds(p, 1), t0:t0 + m]
                        tmp, y = YT[3][:, t0:t0 + m], Y[:, bass.ds(p, 1), t0:t0 + m]
                        link(nc.vector.tensor_scalar(tmp, bank[:, 0:m], RKU[:, RKU_LNG:RKU_LNG + 1], RKU[:, RKU_LNB:RKU_LNB + 1],
                                                     ALU.mult, ALU.add))
                        link.wait()
                        link(nc.vector.tensor_tensor(tmp[:, None, :], tmp[:, None, :], bonus, ALU.add))
                        link.wait()
                        link(nc.vector.tensor_tensor(y, y, tmp[:, None, :], ALU.mult))

        RQ, RKK = U[:, 0:T], U[:, T:2 * T]
        RVT = U[:, 2 * T:3 * T].rearrange("p (c n) -> p c n", c=NCH)
        RKT = U[:, 3 * T:4 * T].rearrange("p (c n) -> p c n", c=NCH)
        V2 = U[:, 4 * T:6 * T].rearrange("p (c d n) -> p c d n", c=NCH, d=2)
        SST = U[:, 6 * T:8 * T].rearrange("p (c d n) -> p c d n", c=NCH, d=2)
        ROPE = U[:, 8 * T:8 * T + 2 * SEQ].rearrange("p (q t) -> p q t", q=2)
        RO = U[:, 10 * T:11 * T].rearrange("p (c n) -> p c n", c=NCH)
        QD = [YT[4], YT[5]]
        DSUM = SL[:, 0:256].rearrange("p (h n) -> p h n", h=2)
        SCR = SL[:, 256:768].rearrange("p (b h n) -> p b h n", b=2, h=2)
        DTMP = SL[:, 768:1280].rearrange("p (m n) -> p m n", m=4)
        QDEC = SL[:, 1280:1536].rearrange("p (d n) -> p d n", d=2)
        LG = SL[:, 1536:1542]
        KDEC = SL[:, 1542:1546]
        CDEC = SL[:, 1546:1548]
        LTMP = SL[:, 1548:1554]

        def ret_project(layer, p):
            dsts = (RQ, RKK, YT[6])
            with Stage(nc, "w_loaded0 w_loaded1 projected taken param_loaded lg_a lg_b lg_c lg "
                           "decays order turned1 turned2 turn_taken swapped swap_taken rotated") as (block, s):
                @block.sync
                def _(sp):
                    sp.dma_start(RTU[:, :], a["rtu"][layer, bass.ds(p, 1)].rearrange("a q n -> q (a n)")
                                 ).then_inc(s["param_loaded"], 16)
                    sp.dma_start(ROPE, a["rope"].rearrange("q p t -> p q t")).then_inc(s["param_loaded"], 16)
                    load_weights(sp, s, W_RT + 4 * p, 4, layer)
                    sp.wait_ge(s["param_loaded"], 32)

                @block.tensor
                def _(pe):
                    for j in range(4):
                        project(pe, s, j)
                    pe.wait_ge(s["taken"], 12)
                    for c in range(NCH):
                        bank, col = (PS[3], c * P) if c < 2 else (PS[4 + (c - 2) // 4], (c - 2) % 4 * P)
                        tr = nc.tensor.transpose(bank[:, col:col + P], YT[6][:, c * P:(c + 1) * P], IDENT)
                    tr.then_inc(s["turned1"], 1)
                    for j, tile in enumerate((RQ, RKK)):
                        if j:
                            pe.wait_ge(s["swap_taken"], 2)
                        for bank, t0, m in pieces()[1:]:
                            mm = nc.tensor.matmul(bank[:, 0:m], cst(C_PERM), tile[:, t0:t0 + m], start=True, stop=True)
                        mm.then_inc(s["swapped"], 1)
                    pe.wait_ge(s["rotated"], 2)
                    pe.wait_ge(s["turn_taken"], 1)
                    for c in range(NCH):
                        bank, col = (PS[3], c * P) if c < 2 else (PS[4 + (c - 2) // 4], (c - 2) % 4 * P)
                        tr = nc.tensor.transpose(bank[:, col:col + P], RKK[:, c * P:(c + 1) * P], IDENT)
                    tr.then_inc(s["turned2"], 1)

                @block.scalar
                def _(act):
                    for j in range(3):
                        for n, (bank, t0, m) in enumerate(pieces()):
                            act.wait_ge(s["projected"], 3 * j + n + 1)
                            nc.scalar.activation(dsts[j][:, t0:t0 + m], bank[:, 0:m], ACT.Copy,
                                                 scale=0.125 if j == 1 else 1.0).then_inc(s["taken"], 1)
                    for n, (bank, t0, m) in enumerate(pieces()):
                        act.wait_ge(s["projected"], 10 + n)
                        nc.scalar.activation(Y[:, bass.ds(2 + p, 1), t0:t0 + m], bank[:, None, 0:m], ACT.Silu
                                             ).then_inc(s["taken"], 1)
                    act.wait_ge(s["param_loaded"], 32)
                    nc.scalar.activation(LTMP, RTU[:, 0:6], ACT.Abs).then_inc(s["lg_a"], 1)
                    act.wait_ge(s["lg_a"], 1)
                    nc.scalar.activation(LTMP, LTMP, ACT.Exp, scale=-1.0).then_inc(s["lg_a"], 1)
                    act.wait_ge(s["lg_a"], 2)
                    nc.scalar.activation(LTMP, LTMP, ACT.Ln, bias=ONE_C).then_inc(s["lg_b"], 1)
                    act.wait_ge(s["lg"], 1)
                    for d in range(2):
                        for h in range(2):
                            m = 2 * d + h
                            nc.scalar.activation(DTMP[:, m, :], cst(C_REL + d * P), ACT.Exp, scale=LG[:, m:m + 1])
                            nc.scalar.activation(KDEC[:, m:m + 1], cst(C_POSC + d, 1), ACT.Exp, scale=LG[:, m:m + 1])
                        nc.scalar.activation(QDEC[:, d, :], cst(C_POSR + d * P), ACT.Exp, scale=LG[:, 4 + d:5 + d])
                    nc.scalar.activation(CDEC, LG[:, 4:6], ACT.Exp, scale=float(CH)).then_inc(s["decays"], 1)
                    for q, sem in enumerate(("turned1", "turned2")):
                        act.wait_ge(s[sem], 1)
                        for bank, t0, m in pieces(3):
                            ins = nc.scalar.copy((RVT, RKT)[q][:, t0 // P:(t0 + m) // P, :],
                                                 bank[:, 0:m].rearrange("p (c n) -> p c n", n=P))
                        ins.then_inc(s["turn_taken"], 1)

                @block.vector
                def _(dve):
                    link = Link(dve, s["order"])
                    dve.wait_ge(s["lg_b"], 1)
                    nc.vector.scalar_tensor_tensor(LG, RTU[:, 0:6], 0.0, LTMP, ALU.min, ALU.subtract).then_inc(s["lg"], 1)
                    for j, tile in enumerate((RQ, RKK)):
                        dve.wait_ge(s["swapped"], j + 1)
                        for bank, t0, m in pieces()[1:]:
                            z, at0 = tile[:, t0:t0 + m], t0 - CTX
                            if t0 > CTX:
                                link.wait()
                            elif j:
                                dve.wait_ge(s["rotated"], j)
                            nc.vector.tensor_tensor(YT[7][:, 0:m], bank[:, 0:m], ROPE[:, 1, at0:at0 + m], ALU.mult
                                                    ).then_inc(s["swap_taken"], 1)
                            link(nc.vector.tensor_tensor(z, z, ROPE[:, 0, at0:at0 + m], ALU.mult))
                            link.wait()
                            dve.wait_ge(s["swap_taken"], 2 * j + (1 if t0 == CTX else 2))
                            if t0 == CTX:
                                link(nc.vector.tensor_tensor(z, z, YT[7][:, 0:m], ALU.add))
                            else:
                                nc.vector.tensor_tensor(z, z, YT[7][:, 0:m], ALU.add).then_inc(s["rotated"], 1)
                    dve.wait_ge(s["decays"], 1)
                    for h in range(2):
                        for d in range(2):
                            link(nc.vector.tensor_tensor(DTMP[:, 2 * d + h, :], DTMP[:, 2 * d + h, :],
                                                         cst(C_SI + d * 256 + P), ALU.mult))
                        link.wait()
                        link(nc.vector.tensor_tensor(DSUM[:, h, :], DTMP[:, h, :], DTMP[:, 2 + h, :], ALU.add))
                    dve.wait_ge(s["rotated"], 2)
                    for d in range(2):
                        link(nc.vector.tensor_tensor(chunked(QD[d]), chunked(RQ), QDEC[:, d, None, :].to_broadcast([P, NCH, P]),
                                                     ALU.mult))
                    dve.wait_ge(s["turn_taken"], 1)
                    for d in range(2):
                        for h in range(2):
                            m, cols = 2 * d + h, slice(64 * h, 64 * h + 64)
                            link(nc.vector.tensor_scalar(V2[:, :, d, cols], RVT[:, :, cols], KDEC[:, m:m + 1], None, ALU.mult))

        def ret_states():
            entering = [[0, 1] + list(range(2, NCH)), [1, 0] + list(range(NCH - 1, 1, -1))]
            with Stage(nc, "kv_done kv_taken order") as (block, s):
                @block.tensor
                def _(pe):
                    for c in range(NCH):
                        if c >= 4:
                            pe.wait_ge(s["kv_taken"], c - 3)
                        nc.tensor.matmul(PS[c % 4][:, 0:256], RKT[:, c, :], V2[:, c].rearrange("p d n -> p (d n)"),
                                         start=True, stop=True).then_inc(s["kv_done"], 1)

                @block.vector
                def _(dve):
                    link = Link(dve, s["order"])
                    for c in range(NCH):
                        dve.wait_ge(s["kv_done"], c + 1)
                        nc.vector.tensor_tensor(V2[:, c], PS[c % 4][:, 0:256].rearrange("p (d n) -> p d n", d=2),
                                                BLK[:, None, :].to_broadcast([P, 2, P]), ALU.mult).then_inc(s["kv_taken"], 1)
                    for d in range(2):
                        link(nc.vector.memset(SST[:, entering[d][0], d, :], 0.0))
                    dve.wait_ge(s["kv_taken"], NCH)
                    for q in range(1, NCH):
                        for d in range(2):
                            c, before = entering[d][q], entering[d][q - 1]
                            dve.wait_ge(s["order"], 2 * q - 1 + d)
                            link(nc.vector.scalar_tensor_tensor(SST[:, c, d, :], SST[:, before, d, :], CDEC[:, d:d + 1],
                                                                V2[:, before, d, :], ALU.mult, ALU.add))

        def ret_outputs():
            with Stage(nc, "scored masked o_done o_taken") as (block, s):
                @block.tensor
                def _(pe):
                    for c in range(NCH + 1):
                        if c < NCH:
                            if c >= 2:
                                pe.wait_ge(s["masked"], c - 1)
                            for h in range(2):
                                rows = slice(64 * h, 64 * h + 64)
                                mm = nc.tensor.matmul(PS[2 * (c % 2) + h][:, 0:P], RKK[rows, c * P:(c + 1) * P],
                                                      RQ[rows, c * P:(c + 1) * P], start=True, stop=True)
                            mm.then_inc(s["scored"], 1)
                        if c:
                            n = c - 1
                            o = PS[4 + n % 2]
                            if n >= 2:
                                pe.wait_ge(s["o_taken"], n - 1)
                            pe.wait_ge(s["masked"], n + 1)
                            for h in range(2):
                                nc.tensor.matmul(o[:, 64 * h:64 * h + 64], SCR[:, n % 2, h, :],
                                                 RVT[:, n, 64 * h:64 * h + 64], start=(h == 0), stop=False,
                                                 skip_group_check=True)
                            for d in range(2):
                                mm = nc.tensor.matmul(o[:, 0:P], QD[d][:, n * P:(n + 1) * P], SST[:, n, d, :],
                                                      start=False, stop=(d == 1), skip_group_check=True)
                            mm.then_inc(s["o_done"], 1)

                @block.vector
                def _(dve):
                    for c in range(NCH):
                        dve.wait_ge(s["scored"], c + 1)
                        if c >= 2:
                            dve.wait_ge(s["o_done"], c - 1)
                        for h in range(2):
                            ins = nc.vector.tensor_tensor(SCR[:, c % 2, h], PS[2 * (c % 2) + h][:, 0:P], DSUM[:, h], ALU.mult)
                        ins.then_inc(s["masked"], 1)

                @block.scalar
                def _(act):
                    for c in range(NCH):
                        act.wait_ge(s["o_done"], c + 1)
                        nc.scalar.copy(RO[:, c, :], PS[4 + c % 2][:, 0:P]).then_inc(s["o_taken"], 1)

        def ret_post(p):
            with Stage(nc, "var_ready rstd_ready o_ready turned order") as (block, s):
                heads = lambda x: x.rearrange("p c (h n) -> p c h n", h=2)
                rstd = normalise_heads(block, s, None, None, heads(RO), heads(V2[:, :, 0, :]), 2, False, EPS_C)

                @block.scalar
                def _(act):
                    rstd(act)

                @block.tensor
                def _(pe):
                    pe.wait_ge(s["o_ready"], 1)
                    turn_outputs(pe, s, RO, None)
            with Stage(nc, "order") as (block, s):
                @block.vector
                def _(dve):
                    for bank, t0, m in pieces():
                        y = Y[:, bass.ds(2 + p, 1), t0:t0 + m]
                        nc.vector.scalar_tensor_tensor(y, bank[:, None, 0:m], RTU[:, RTU_G:RTU_G + 1], y, ALU.mult, ALU.mult)

        def gdn_scalars(layer):
            ab = U[:, 0:NCH * 16].rearrange("p (c q k) -> p c q k", c=NCH, q=2)
            sp_in, mag, rest = (U[:, 200 + 80 * q:280 + 80 * q].rearrange("p (c k) -> p c k", c=NCH) for q in range(3))
            wab = W[:, 0, 0:KT * 16].rearrange("p (k n) -> p k n", k=KT)
            nea = GP[:, 0, :]

            def gs(q):
                return GS[:, :, :, :, q].rearrange("p c h d -> p c (h d)")

            with Stage(nc, "w_loaded0 projected x_ready steps act_steps g_ready summed order") as (block, s):
                @block.sync
                def _(sp):
                    sp.dma_start(wab, a["w_ab"][layer]).then_inc(s["w_loaded0"], 16)

                @block.tensor
                def _(pe):
                    pe.wait_ge(s["w_loaded0"], 16)
                    for c in range(NCH):
                        for k in range(KT):
                            mm = nc.tensor.matmul(PS[0][:, c * 16:(c + 1) * 16], H[:, k, c * P:(c + 1) * P], wab[:, k, :],
                                                  start=(k == 0), stop=(k == KT - 1))
                    mm.then_inc(s["projected"], 1)
                    pe.wait_ge(s["g_ready"], 1)
                    for d in range(2):
                        nc.tensor.matmul(PS[1][:, 80 * d:80 * d + 80], cst(C_SI + d * 256 + P), rest.rearrange("p c k -> p (c k)"),
                                         start=True, stop=True)
                    nc.tensor.matmul(PS[1][:, 160:240], ONES, rest.rearrange("p c k -> p (c k)"),
                                     start=True, stop=True).then_inc(s["summed"], 1)

                @block.scalar
                def _(act):
                    nc.scalar.activation(nea, nea, ACT.Exp).then_inc(s["act_steps"], 1)
                    act.wait_ge(s["x_ready"], 1)
                    nc.scalar.activation(mag, sp_in, ACT.Abs).then_inc(s["act_steps"], 1)
                    act.wait_ge(s["act_steps"], 2)
                    nc.scalar.activation(mag, mag, ACT.Exp, scale=-1.0).then_inc(s["act_steps"], 1)
                    act.wait_ge(s["act_steps"], 3)
                    nc.scalar.activation(mag, mag, ACT.Ln, bias=ONE_C).then_inc(s["act_steps"], 1)
                    nc.scalar.activation(gs(G_BETA), ab[:, :, 1, :], ACT.Sigmoid)
                    act.wait_ge(s["steps"], 1)
                    nc.scalar.activation(gs(G_EG), gs(G_NGC), ACT.Exp, scale=-1.0).then_inc(s["act_steps"], 1)
                    nc.scalar.activation(gs(G_WK), gs(G_WK), ACT.Exp)
                    nc.scalar.activation(gs(G_CD), PS[1][:, 160:240].rearrange("p (c k) -> p c k", c=NCH), ACT.Exp)

                @block.vector
                def _(dve):
                    link = Link(dve, s["order"])
                    dve.wait_ge(s["projected"], 1)
                    link(nc.vector.tensor_copy(ab, PS[0][:, 0:160].rearrange("p (c q k) -> p c q k", c=NCH, q=2)))
                    link.wait()
                    nc.vector.tensor_tensor(sp_in, ab[:, :, 0, :], GP[:, 1, None, :].to_broadcast([P, NCH, 8]), ALU.add
                                            ).then_inc(s["x_ready"], 1)
                    dve.wait_ge(s["act_steps"], 4)
                    link(nc.vector.scalar_tensor_tensor(sp_in, sp_in, 0.0, mag, ALU.max, ALU.add))
                    link.wait()
                    link(nc.vector.tensor_tensor(sp_in, sp_in, nea[:, None, :].to_broadcast([P, NCH, 8]), ALU.mult))
                    link.wait()
                    nc.vector.tensor_scalar(rest, sp_in, -1.0, -104.0, ALU.mult, ALU.max).then_inc(s["g_ready"], 1)
                    dve.wait_ge(s["g_ready"], 1)
                    link(nc.vector.tensor_copy(gs(G_G), rest))
                    dve.wait_ge(s["summed"], 1)
                    for d in range(2):
                        mine = PS[1][:, 80 * d:80 * d + 80].rearrange("p (c h d) -> p c h d", c=NCH, d=2)[:, :, :, d]
                        link(nc.vector.tensor_scalar(GS[:, :, :, d, G_NGC], mine, -1.0, None, ALU.mult))
                    link.wait()
                    nc.vector.tensor_tensor(gs(G_WK), gs(G_NGC), PS[1][:, 160:240].rearrange("p (c k) -> p c k", c=NCH), ALU.add
                                            ).then_inc(s["steps"], 1)
                    dve.wait_ge(s["act_steps"], 5)
                    nc.vector.tensor_scalar(gs(G_NEG), gs(G_EG), -1.0, None, ALU.mult)

        KQ = U[:, 0:4 * T].rearrange("p (h q t) -> p h q t", h=2, q=2)
        GVT = U[:, 4 * T:6 * T].rearrange("p (c h n) -> p c h n", c=NCH, h=2)
        GO = U[:, 6 * T:10 * T].rearrange("p (d c h n) -> p d c h n", d=2, c=NCH, h=2)
        TMP = [U[:, (6 + q) * T:(7 + q) * T] for q in range(4)]

        def gdn_project(layer, u):
            dsts = [KQ[:, 0, 0, :], KQ[:, 1, 0, :], KQ[:, 0, 1, :], KQ[:, 1, 1, :], TMP[0], TMP[1]]
            with Stage(nc, "w_loaded0 w_loaded1 projected taken convolved param_loaded silu order pads "
                           "turned turn_taken squared summed ln_done rstd_ready scaled") as (block, s):
                @block.sync
                def _(sp):
                    sp.dma_start(GDU[:, :], a["gdu"][layer]).then_inc(s["param_loaded"], 16)
                    load_weights(sp, s, W_GD + 8 * u, 8, layer)
                    sp.wait_ge(s["param_loaded"], 16)

                @block.gpsimd
                def _(pool):
                    for col in (0, CTX + 1, CTX + 2, T + 3):
                        ins = nc.gpsimd.memset(RAW[:, col:col + 1], 0.0)
                    ins.then_inc(s["pads"], 1)

                @block.tensor
                def _(pe):
                    for j in range(8):
                        project(pe, s, j)
                    pe.wait_ge(s["silu"], 6)
                    for h in range(2):
                        if h:
                            pe.wait_ge(s["turn_taken"], 1)
                        for c in range(NCH):
                            bank, col = (PS[3], c * P) if c < 2 else (PS[4 + (c - 2) // 4], (c - 2) % 4 * P)
                            tr = nc.tensor.transpose(bank[:, col:col + P], TMP[h][:, c * P:(c + 1) * P], IDENT)
                        tr.then_inc(s["turned"], 1)
                    pe.wait_ge(s["taken"], 24)
                    for j in range(4):
                        pe.wait_ge(s["squared"], j + 1)
                        if j:
                            pe.wait_ge(s["ln_done"], j)
                        column_sums(pe, TMP[2 + j % 2], ONES).then_inc(s["summed"], 1)

                @block.scalar
                def _(act):
                    for j in range(8):
                        h = j % 2
                        for n, (bank, t0, m) in enumerate(pieces()):
                            act.wait_ge(s["projected"], 3 * j + n + 1)
                            if j < 6:
                                if n == 0 and j:
                                    act.wait_ge(s["convolved"], j)
                                if n == 0:
                                    act.wait_ge(s["pads"], 1)
                                nc.scalar.copy(raw_of(t0, m), bank[:, 0:m]).then_inc(s["taken"], 1)
                            else:
                                nc.scalar.activation(Y[:, bass.ds(4 + 2 * u + h, 1), t0:t0 + m], bank[:, None, 0:m], ACT.Silu
                                                     ).then_inc(s["taken"], 1)
                        if 1 <= j <= 6:
                            act.wait_ge(s["convolved"], j)
                            nc.scalar.activation(dsts[j - 1], dsts[j - 1], ACT.Silu).then_inc(s["silu"], 1)
                    for h in range(2):
                        act.wait_ge(s["turned"], h + 1)
                        for bank, t0, m in pieces(3):
                            ins = nc.scalar.copy(GVT[:, t0 // P:(t0 + m) // P, h, :], bank[:, 0:m].rearrange("p (c n) -> p c n", n=P))
                        ins.then_inc(s["turn_taken"], 1)
                    for j in range(4):
                        act.wait_ge(s["summed"], j + 1)
                        t = TMP[j % 2]
                        if j >= 2:
                            act.wait_ge(s["scaled"], j - 1)
                        for bank, t0, m in pieces():
                            ins = nc.scalar.activation(t[:, t0:t0 + m], bank[:, 0:m], ACT.Ln, bias=EPS_C)
                        ins.then_inc(s["ln_done"], 1)
                        act.wait_ge(s["ln_done"], j + 1)
                        if j < 2:
                            nc.scalar.activation(t, t, ACT.Exp, scale=-0.5).then_inc(s["rstd_ready"], 1)
                        else:
                            nc.scalar.activation(t, t, ACT.Exp, scale=-0.5, bias=HALFLN_C).then_inc(s["rstd_ready"], 1)

                @block.vector
                def _(dve):
                    link = Link(dve, s["order"])
                    dve.wait_ge(s["param_loaded"], 16)
                    cols = RKU[:, 0:18]
                    for j in range(6):
                        dve.wait_ge(s["taken"], 3 * (j + 1))

                        def tap(q):
                            return RKU[:, 3 * j + q:3 * j + q + 1]

                        if j == 0:
                            link(nc.vector.tensor_copy(cols[:, None, :], GDU[:, :].rearrange("p (u n) -> p u n", u=2)[:, bass.ds(u, 1), 0:18]))
                            link.wait()
                        ranges = ((0, CTX, 0), (CTX, T, CTX + 2))
                        for t0, t1, r in ranges:
                            link(nc.vector.tensor_scalar(dsts[j][:, t0:t1], RAW[:, r:r + t1 - t0], tap(0), None, ALU.mult))
                        for q in (1, 2):
                            link.wait()
                            for t0, t1, r in ranges:
                                ins = nc.vector.scalar_tensor_tensor(dsts[j][:, t0:t1], RAW[:, r + q:r + q + t1 - t0], tap(q),
                                                                     dsts[j][:, t0:t1], ALU.mult, ALU.add)
                                if q == 2 and t1 == T:
                                    ins.then_inc(s["convolved"], 1)
                                else:
                                    link(ins)
                    for j in range(6):
                        if j < 4:
                            dve.wait_ge(s["silu"], j + 1)
                            if j >= 2:
                                dve.wait_ge(s["summed"], j - 1)
                            nc.vector.tensor_tensor(TMP[2 + j % 2], dsts[j], dsts[j], ALU.mult).then_inc(s["squared"], 1)
                        if j >= 2:
                            dve.wait_ge(s["rstd_ready"], j - 1)
                            nc.vector.tensor_tensor(dsts[j - 2], dsts[j - 2], TMP[j % 2], ALU.mult).then_inc(s["scaled"], 1)

        GM, EM, ESM, UT, AT, VD, VN, VK = (SL[:, 512 * q:512 * (q + 1)].rearrange("p (m n) -> p m n", m=4) for q in range(8))
        OS = GM
        KQS = SLOT[:, :].rearrange("p (d h q n) -> p d h q n", d=2, h=2, q=2)
        KT4 = KTOK[:, :].rearrange("p (m n) -> p m n", m=4)
        GST = STATE[:, :].rearrange("p (m n) -> p m n", m=4)

        def gdn_init(u):
            def init():
                with Stage(nc, "order") as (block, s):
                    @block.vector
                    def _(dve):
                        nc.vector.memset(GST, 0.0)
                        nc.vector.tensor_copy(GSU[:, :, :, :, :].rearrange("p c h d q -> p c (h d q)"),
                                              GS[:, :, bass.ds(2 * u, 2), :, :].rearrange("p c h d q -> p c (h d q)"))
            return init

        def gdn_step(cf, cb, nf, nb):
            def col(m, q):
                return SC[:, m // 2, m % 2, q:q + 1]

            def wide(q):
                return SC[:, :, :, q:q + 1].rearrange("p d h q -> p (d h) q").to_broadcast([P, 4, P])

            def bank4(b):
                return PS[b][:, :].rearrange("p (m n) -> p m n", m=4)

            with Stage(nc, SOLVER + "slots_ready sc_ready gm_ready gated clamped decayed es_ready em_ready ut_raw at_ready "
                           "ks_scored turned turn_taken ks_done vd_ready w_done vn_ready vk_ready os_ready av_done kv_done "
                           "order") as (block, s):
                @block.scalar
                def _(act):
                    for d, c in enumerate((cf, cb)):
                        tok = c * P if isinstance(c, int) else c * P
                        nc.scalar.copy(KQS[:, d].rearrange("p h q n -> p (h q) n"),
                                       KQ[:, :, :, bass.ds(tok, P)].rearrange("p h q t -> p (h q) t")).then_inc(s["slots_ready"], 1)
                    act.wait_ge(s["clamped"], 1)
                    nc.scalar.activation(EM, EM, ACT.Exp).then_inc(s["decayed"], 1)
                    act.wait_ge(s["turned"], 1)
                    nc.scalar.copy(KT4, bank4(3)).then_inc(s["turn_taken"], 1)
                    solve_scalar(act, s)

                @block.gpsimd
                def _(pool):
                    pool.wait_ge(s["decayed"], 1)
                    for d in range(2):
                        ins = nc.gpsimd.tensor_tensor(ESM[:, 2 * d:2 * d + 2, :], EM[:, 2 * d:2 * d + 2, :],
                                                      CST[:, None, C_SI + d * 256:C_SI + d * 256 + P].to_broadcast([P, 2, P]), ALU.mult)
                    ins.then_inc(s["es_ready"], 1)
                    pool.wait_ge(s["es_ready"], 1)
                    nc.gpsimd.tensor_tensor(EM, ESM, IDENT[:, None, :].to_broadcast([P, 4, P]), ALU.add).then_inc(s["em_ready"], 1)
                    pool.wait_ge(s["ut_raw"], 1)
                    nc.gpsimd.tensor_tensor(UT, UT, IDENT[:, None, :].to_broadcast([P, 4, P]), ALU.add).then_inc(s["ut_ready"], 1)
                    pool.wait_ge(s["vn_ready"], 1)
                    nc.gpsimd.tensor_tensor(VK, VN, wide(G_WK), ALU.mult).then_inc(s["vk_ready"], 1)

                @block.tensor
                def _(pe):
                    pe.wait_ge(s["gm_ready"], 1)
                    nc.tensor.matmul(PS[2][:, :], ONES, GM.rearrange("p m n -> p (m n)"), start=True, stop=True).then_inc(s["gated"], 1)
                    for d in range(2):
                        pe.wait_ge(s["slots_ready"], d + 1)
                        for h in range(2):
                            mm = nc.tensor.matmul(PS[d][:, 256 * h:256 * h + 256], KQS[:, d, h, 0, :], KQS[:, d, h, :, :].rearrange("p q n -> p (q n)"),
                                                  start=True, stop=True)
                    mm.then_inc(s["ks_scored"], 1)
                    for m in range(4):
                        mm = nc.tensor.transpose(PS[3][:, m * P:(m + 1) * P], KQS[:, m // 2, m % 2, 0, :], IDENT)
                    mm.then_inc(s["turned"], 1)
                    pe.wait_ge(s["ut_ready"], 1)
                    solve_tensor(pe, s, lambda m: UT[:, m, :])
                    for m in range(4):
                        nc.tensor.matmul(PS[7][:, m * P:(m + 1) * P], KQS[:, m // 2, m % 2, 0, :], GST[:, m, :], start=True, stop=True)
                    for m in range(4):
                        mm = nc.tensor.matmul(PS[0][:, m * P:(m + 1) * P], KQS[:, m // 2, m % 2, 1, :], GST[:, m, :], start=True, stop=True)
                    mm.then_inc(s["ks_done"], 1)
                    pe.wait_ge(s["vd_ready"], 1)
                    pe.wait_ge(s["y_taken"], LEVELS)
                    for m in range(4):
                        mm = nc.tensor.matmul(PS[1][:, m * P:(m + 1) * P], YS[:, m, :], VD[:, m, :], start=True, stop=True)
                    mm.then_inc(s["w_done"], 1)
                    pe.wait_ge(s["vn_ready"], 1)
                    for m in range(4):
                        mm = nc.tensor.matmul(PS[2][:, m * P:(m + 1) * P], AT[:, m, :], VN[:, m, :], start=True, stop=True)
                    mm.then_inc(s["av_done"], 1)
                    pe.wait_ge(s["vk_ready"], 1)
                    for m in range(4):
                        mm = nc.tensor.matmul(PS[3][:, m * P:(m + 1) * P], KT4[:, m, :], VK[:, m, :], start=True, stop=True)
                    mm.then_inc(s["kv_done"], 1)

                @block.vector
                def _(dve):
                    link = Link(dve, s["order"])
                    for d, c in enumerate((cf, cb)):
                        link(nc.vector.tensor_copy(SC[:, d:d + 1], GSU[:, at(c), :, d, :]))
                    link.wait()
                    for m in range(4):
                        ins = nc.vector.tensor_scalar(GM[:, m, :], cst(C_SI + (m // 2) * 256 + P), col(m, G_G), None, ALU.mult)
                    ins.then_inc(s["gm_ready"], 1)
                    dve.wait_ge(s["gated"], 1)
                    for m in range(4):
                        ins = nc.vector.tensor_scalar(EM[:, m, :], PS[2][:, m * P:(m + 1) * P], col(m, G_NGC), 0.0, ALU.add, ALU.min)
                    ins.then_inc(s["clamped"], 1)
                    dve.wait_ge(s["ks_scored"], 1)
                    dve.wait_ge(s["es_ready"], 1)
                    for m in range(4):
                        b = PS[m // 2][:, 256 * (m % 2):256 * (m % 2) + P]
                        ins = nc.vector.scalar_tensor_tensor(UT[:, m, :], b, col(m, G_BETA), ESM[:, m, :], ALU.mult, ALU.mult)
                    ins.then_inc(s["ut_raw"], 1)
                    dve.wait_ge(s["em_ready"], 1)
                    for d in range(2):
                        ins = nc.vector.tensor_tensor(AT[:, 2 * d:2 * d + 2, :], PS[d][:, :].rearrange("p (h q n) -> p h q n", h=2, q=2)[:, :, 1, :],
                                                      EM[:, 2 * d:2 * d + 2, :], ALU.mult)
                    ins.then_inc(s["at_ready"], 1)
                    dve.wait_ge(s["ut_ready"], 1)
                    solve_vector(dve, s, lambda d: UT[:, 2 * d:2 * d + 2, :])
                    dve.wait_ge(s["ks_done"], 1)
                    for m in range(4):
                        v = GVT[:, at((cf, cb)[m // 2]), m % 2, :]
                        ins = nc.vector.scalar_tensor_tensor(VD[:, m:m + 1, :], PS[7][:, None, m * P:(m + 1) * P], col(m, G_NEG), v,
                                                             ALU.mult, ALU.add)
                    ins.then_inc(s["vd_ready"], 1)
                    nc.vector.tensor_tensor(OS, bank4(0), wide(G_EG), ALU.mult).then_inc(s["os_ready"], 1)
                    dve.wait_ge(s["w_done"], 1)
                    nc.vector.tensor_tensor(VN, bank4(1), wide(G_BETA), ALU.mult).then_inc(s["vn_ready"], 1)
                    dve.wait_ge(s["av_done"], 1)
                    dve.wait_ge(s["os_ready"], 1)
                    for d, c in enumerate((cf, cb)):
                        nc.vector.tensor_tensor(GO[:, d, at(c)].rearrange("p c h n -> p c (h n)"),
                                                PS[2][:, None, 256 * d:256 * d + 256],
                                                OS[:, 2 * d:2 * d + 2, :].rearrange("p (o h) n -> p o (h n)", o=1), ALU.add)
                    dve.wait_ge(s["kv_done"], 1)
                    for m in range(4):
                        nc.vector.scalar_tensor_tensor(GST[:, m, :], GST[:, m, :], col(m, G_CD), PS[3][:, m * P:(m + 1) * P],
                                                       ALU.mult, ALU.add)

        def gdn_post(u):
            for h in range(2):
                o = GO[:, 0, :, h:h + 1, :]
                with Stage(nc, "var_ready rstd_ready o_ready turned order") as (block, s):
                    rstd = normalise_heads(block, s, o, GO[:, 1, :, h:h + 1, :], o, KQ[:, 0, 0, :].rearrange(
                        "p (c h n) -> p c h n", c=NCH, h=1), 1, False, EPS_C)

                    @block.scalar
                    def _(act):
                        rstd(act)

                    @block.tensor
                    def _(pe):
                        pe.wait_ge(s["o_ready"], 1)
                        turn_outputs(pe, s, GO[:, 0, :, h, :], None)
                with Stage(nc, "order") as (block, s):
                    @block.vector
                    def _(dve):
                        for bank, t0, m in pieces():
                            y = Y[:, bass.ds(4 + 2 * u + h, 1), t0:t0 + m]
                            nc.vector.scalar_tensor_tensor(y, bank[:, None, 0:m], GDU[:, GDU_G:GDU_G + 1], y, ALU.mult, ALU.mult)

        def project_out(layer, last):
            src = a["xT"] if layer == 0 else x_next
            part = pieces()[1:] if last else pieces()
            with nc.Fori(0, KT // 2) as i:
                with Stage(nc, "w_loaded0 w_loaded1 x_loaded0 x_loaded1 projected summed stored") as (block, s):
                    XO = [U[:, 0:T], U[:, T:2 * T]]

                    @block.sync
                    def _(sp):
                        for q in range(2):
                            sp.dma_start(W[:, q, :], a["w_o"][layer, bass.ds(2 * i + q, 1)].rearrange("a p n -> p (a n)")
                                         ).then_inc(s[f"w_loaded{q}"], 16)
                            sp.dma_start(XO[q], src[bass.ds(2 * i + q, 1)].rearrange("a p t -> p (a t)")).then_inc(s[f"x_loaded{q}"], 16)
                        sp.wait_ge(s["w_loaded0"], 16)
                        sp.wait_ge(s["x_loaded0"], 16)
                        if not last:
                            for q in range(2):
                                sp.wait_ge(s["summed"], len(part) * (q + 1))
                                sp.dma_start(x_next[bass.ds(2 * i + q, 1)].rearrange("a p t -> p (a t)"), XO[q]).then_inc(s["stored"], 16)
                            sp.wait_ge(s["stored"], 32)

                    @block.tensor
                    def _(pe):
                        for q in range(2):
                            pe.wait_ge(s[f"w_loaded{q}"], 16)
                            for n, (_, t0, m) in enumerate(part):
                                bank = PS[3 * q + n]
                                for k in range(KT):
                                    mm = nc.tensor.matmul(bank[:, 0:m], W[:, q, k * P:(k + 1) * P], Y[:, k, t0:t0 + m],
                                                          start=(k == 0), stop=(k == KT - 1))
                                mm.then_inc(s["projected"], 1)

                    @block.vector
                    def _(dve):
                        for q in range(2):
                            dve.wait_ge(s[f"x_loaded{q}"], 16)
                            for n, (_, t0, m) in enumerate(part):
                                v = 1 if t0 < CTX else 0
                                dve.wait_ge(s["projected"], len(part) * q + n + 1)
                                x = XO[q][:, t0:t0 + m]
                                nc.vector.scalar_tensor_tensor(x[:, None, :], PS[3 * q + n][:, None, 0:m],
                                                               MOD[:, bass.ds(16 + 2 * i + q, 1), v], x[:, None, :],
                                                               ALU.mult, ALU.add).then_inc(s["summed"], 1)

                    @block.scalar
                    def _(act):
                        for q in range(2):
                            act.wait_ge(s["summed"], len(part) * (q + 1))
                            t0 = part[0][1]
                            nc.scalar.copy(H[:, bass.ds(2 * i + q, 1), t0:T], XO[q][:, None, t0:T])

        for layer in range(DEPTH):
            modulation(layer)
            normalise()
            rwkv_common(layer)
            with nc.Fori(0, 2) as p:
                rwkv_project(layer, p)
                for d in range(2):
                    rwkv_packages(p, d)
                scan(rwkv_step, rwkv_init)
                rwkv_post(p)
            with nc.Fori(0, 2) as p:
                ret_project(layer, p)
                ret_states()
                ret_outputs()
                ret_post(p)
            gdn_scalars(layer)
            with nc.Fori(0, 2) as u:
                gdn_project(layer, u)
                scan(gdn_step, gdn_init(u))
                gdn_post(u)
            project_out(layer, layer == DEPTH - 1)

        with Stage(nc, "squared summed rstd_ready act_order order ready stored") as (block, s):
            mean_square(block, s)

            @block.vector
            def _(dve):
                dve.wait_ge(s["rstd_ready"], 1)
                for k in range(KT):
                    nc.vector.scalar_tensor_tensor(H[:, k, CTX:T], H[:, k, CTX:T], FG[:, k:k + 1], RSTD[:, CTX:T],
                                                   ALU.mult, ALU.mult).then_inc(s["ready"], 1)

            @block.sync
            def _(sp):
                for k in range(KT):
                    sp.wait_ge(s["ready"], k + 1)
                    sp.dma_start(out[k], H[:, k, CTX:T]).then_inc(s["stored"], 16)
                sp.wait_ge(s["stored"], 16 * KT)


def pack(x, c, ctx, c_ctx, ada_w, ada_b, norm_g, w_in, w_out, rk_mu, rk_w0, rk_w2, rk_a0, rk_a2, rk_kk, rk_ka, rk_rk,
         rk_v0, rk_v1, rk_v2, rk_ln_g, rk_ln_b, ret_decay, ret_norm_g, gdn_conv, gdn_a_log, gdn_dt_bias, gdn_norm_g, final_g):
    L = DEPTH

    def cols(v):
        return v.reshape(v.shape[0], -1, P).transpose(0, 2, 1)

    def tile(start):
        return list(range(start, start + P))

    order = [tile(512), tile(640), tile(768)]
    for p in range(2):
        order += [tile(128 * p), tile(256 + 128 * p), tile(896 + 128 * p)]
    for p in range(2):
        order += [tile(1152 + 256 * q + 128 * p) for q in range(4)]
    for u in range(2):
        order += [tile(2176 + 512 * q + 128 * (2 * u + h)) for q in (1, 0, 2, 3) for h in range(2)]
    order = np.array(order)
    w = w_in.reshape(L, KT, P, N_IN)
    w_t = w[:, :, :, order.ravel()].reshape(L, KT, P, N_WT, P).transpose(0, 3, 2, 1, 4).reshape(L, N_WT, P, KT * P)
    ab = np.array([4224 + 8 * kind + 4 * d + h for kind in range(2) for h in range(4) for d in range(2)])
    w_ab = w[:, :, :, ab].transpose(0, 2, 1, 3)
    rkc = np.zeros((L, P, N_RKC), np.float32)
    rkc[:, :, 0:3] = cols(rk_mu)[:, :, 4:7]
    rkc[1:, :, RKC_V0:RKC_V1] = cols(rk_v0)
    rkc[1:, :, RKC_V1:RKC_V2] = rk_v1.reshape(L - 1, 2, P, 32).transpose(0, 2, 1, 3).reshape(L - 1, P, 64)
    rkc[1:, 0:32, RKC_V2:N_RKC] = rk_v2
    rku = np.zeros((L, 2, P, N_RKU), np.float32)
    rku[:, :, 0:64, 0:256] = rk_w2.reshape(L, 2, 64, 2, P).transpose(0, 3, 2, 1, 4).reshape(L, 2, 64, 256)
    rku[:, :, 64:128, 0:256] = rk_a2.reshape(L, 2, 64, 2, P).transpose(0, 3, 2, 1, 4).reshape(L, 2, 64, 256)
    rku[:, :, :, RKU_W0:RKU_A0] = rk_w0.reshape(L, 2, 2, P).transpose(0, 2, 3, 1)
    rku[:, :, :, RKU_A0:RKU_KK] = rk_a0.reshape(L, 2, 2, P).transpose(0, 2, 3, 1)
    for at, v in ((RKU_KK, rk_kk), (RKU_KA, rk_ka), (RKU_RK, rk_rk.reshape(L, -1)), (RKU_LNG, rk_ln_g), (RKU_LNB, rk_ln_b),
                  (RKU_MU, rk_mu[:, 0:256]), (RKU_MU + 1, rk_mu[:, 256:512])):
        rku[:, :, :, at] = v.reshape(L, 2, P)
    rtu = np.zeros((L, 2, P, N_RTU), np.float32)
    by_pair = ret_decay.reshape(L, 2, 2, 2)
    rtu[:, :, :, 0:4] = by_pair.transpose(0, 2, 1, 3).reshape(L, 2, 1, 4)
    rtu[:, :, :, 4:6] = np.repeat(by_pair.transpose(0, 2, 3, 1), 64, axis=2)
    rtu[:, :, :, RTU_G] = ret_norm_g.reshape(L, 2, P)
    conv = gdn_conv.reshape(L, 3, 3, 4, P)
    gdu = np.zeros((L, P, 2, N_GDU), np.float32)
    for u in range(2):
        for j, q in enumerate((1, 0, 2)):
            for h in range(2):
                gdu[:, :, u, 3 * (2 * j + h):3 * (2 * j + h) + 3] = conv[:, :, q, 2 * u + h, :].transpose(0, 2, 1)
        gdu[:, :, u, GDU_G] = gdn_norm_g
    gda = np.stack([gdn_a_log.transpose(0, 2, 1).reshape(L, 8), gdn_dt_bias.transpose(0, 2, 1).reshape(L, 8)], 1)
    out = {
        "xT": np.concatenate([ctx[0], x[0]], 0).T.reshape(KT, P, T),
        "cc": np.stack([c[0], c_ctx], -1).reshape(KT, P, 2).transpose(1, 0, 2),
        "ada_w": ada_w.reshape(L, KT, P, 8, 384).transpose(0, 3, 2, 1, 4),
        "ada_b": cols(ada_b), "norm_g": cols(norm_g), "final_g": cols(final_g[None])[0],
        "w_t": w_t, "w_ab": w_ab,
        "w_o": w_out.reshape(L, KT, P, KT, P).transpose(0, 3, 2, 1, 4).reshape(L, KT, P, KT * P),
        "rkc": rkc, "rku": rku, "rtu": rtu, "gdu": gdu.reshape(L, P, 2 * N_GDU),
        "gda": np.broadcast_to(gda[:, None], (L, P, 2, 8)),
        "consts": constants(), "rope": rope_tables(),
    }
    return {k: np.ascontiguousarray(v) for k, v in out.items()}


def kernel(**inputs):
    import concourse.bacc as bacc
    from concourse.bass_utils import run_bass_kernel_spmd

    nc = bacc.Bacc("TRN2", target_bir_lowering=False, num_devices=1)
    arrays = pack(**{k: np.asarray(v) for k, v in inputs.items()})
    aps = {k: nc.dram_tensor(k + "_in", v.shape, F32, kind="ExternalInput").ap() for k, v in arrays.items()}
    out = nc.dram_tensor("latents_out", (KT, P, SEQ), F32, kind="ExternalOutput").ap()
    build(nc, aps, out)
    r = run_bass_kernel_spmd(nc, [{k + "_in": v for k, v in arrays.items()}], core_ids=[0])
    return r.results[0]["latents_out"].reshape(1, D, SEQ).transpose(0, 2, 1)
```

```python
from contextlib import ExitStack
import math

import concourse.bass as bass
import numpy as np
from concourse import mybir

F32 = mybir.dt.float32
I32 = mybir.dt.int32
ALU = mybir.AluOpType
ACT = mybir.ActivationFunctionType
AX = mybir.AxisListType.X

P = 128
D = 1024
KT = D // P
CTX = 256
SEQ = 1024
T = CTX + SEQ
CH = 128
NC_CTX = CTX // CH
NCH = T // CH
GRID = 64
DEPTH = 2
N_IN = 4240
PIECES = ((0, CTX), (CTX, 512), (CTX + 512, 512))
LEVELS = 7
EPS = 1e-6
LN_EPS = 64e-5
NEG_SQRT_E = -math.exp(-0.5)

C_IDENT, C_ONES, C_BLK, C_PERM = 0, 128, 256, 384
C_LVL = 512
C_SI = C_LVL + LEVELS * 2 * 128
C_REL = C_SI + 512
C_POSR = C_REL + 256
C_POSC = C_POSR + 256
C_TYPE = C_POSC + 2
N_CST = C_TYPE + 4

W_RK_COMMON, W_RK, W_RT, W_GD, N_WT = 0, 3, 9, 17, 33

RKC_MU, RKC_V0, RKC_V1, RKC_V2, N_RKC = 0, 3, 5, 69, 325
RKU_LORA, RKU_W0, RKU_A0, RKU_KK, RKU_KA, RKU_RK, RKU_LNG, RKU_LNB, RKU_MU, N_RKU = 0, 512, 514, 516, 517, 518, 519, 520, 521, 523
RTU_ROW, RTU_COL, RTU_G, N_RTU = 0, 4, 6, 7
GDU_CONV, GDU_G, N_GDU = 0, 18, 19
G_G, G_NGC, G_BETA, G_NEG, G_EG, G_WK, G_CD, N_GS = 0, 1, 2, 3, 4, 5, 6, 7


def constants():
    c = np.zeros((P, N_CST), np.float32)
    j, i = np.arange(P)[:, None], np.arange(P)[None, :]
    c[:, C_IDENT:C_IDENT + P] = j == i
    c[:, C_ONES:C_ONES + P] = 1
    c[:, C_BLK:C_BLK + P] = j // 64 == i // 64
    c[:, C_PERM:C_PERM + P] = np.where((i % 64 < 32) & (j == i + 32), -1, 0) + np.where((i % 64 >= 32) & (j == i - 32), 1, 0)
    for lv in range(LEVELS):
        b = 1 << lv
        same = j // (2 * b) == i // (2 * b)
        for d, (row, col) in enumerate(((j, i), (i, j))):
            block = same & (row % (2 * b) >= b) & (col % (2 * b) < b)
            at = C_LVL + (lv * 2 + d) * P
            c[:, at:at + P] = np.where(j == i, 1, 0) - np.where(block, 1, 0)
    for d, (first, then) in enumerate(((j, i), (i, j))):
        at = C_SI + d * 256
        c[:, at:at + P] = first < then
        c[:, at + P:at + 2 * P] = first <= then
        c[:, C_REL + d * P:C_REL + (d + 1) * P] = np.maximum(then - first, 0)
        c[:, C_POSR + d * P:C_POSR + (d + 1) * P] = (i + 1) if d == 0 else (P - i)
        c[:, C_POSC + d] = (P - 1 - j[:, 0]) if d == 0 else j[:, 0]
    for s in range(4):
        c[:, C_TYPE + s] = j[:, 0] % 4 == s
    return c


def rope_tables():
    n_freq = 16
    inv = np.float32(10000.0) ** (-np.arange(n_freq, dtype=np.float32) / np.float32(n_freq))
    t = np.arange(SEQ)
    ang = np.concatenate([(t // GRID).astype(np.float32)[:, None] * inv, (t % GRID).astype(np.float32)[:, None] * inv], -1)
    ang = np.concatenate([ang] * 4, -1).T
    return np.ascontiguousarray(np.stack([np.cos(ang), np.sin(ang)]).astype(np.float32))


class Stage:
    used = []

    def __init__(self, nc, names):
        self.nc, self.names, self.ctx = nc, names.split(), ExitStack()

    def __enter__(self):
        self.turn = 1 - Stage.used[0].turn if Stage.used else 0
        self.s = {n: self.ctx.enter_context(self.nc.semaphore(f"{n}_{'ab'[self.turn]}")) for n in self.names}
        self.block_guard = self.nc.Block()
        self.block = self.block_guard.__enter__()
        return self.block, self.s

    def __exit__(self, *exc):
        if exc[0] is None and Stage.used:
            before = Stage.used[0].s

            @self.block.sync
            def _(sp):
                for n in before:
                    sp.sem_clear(before[n])
        self.block_guard.__exit__(*exc)
        if exc[0] is None:
            if Stage.used:
                Stage.used.pop().ctx.close()
            Stage.used.append(self)


def settle(nc):
    last = Stage.used.pop()
    with nc.Block() as block:
        @block.sync
        def _(sp):
            for n in last.s:
                sp.sem_clear(last.s[n])
    last.ctx.close()


class StepStage:

    def __init__(self, nc, sets, turn):
        self.nc, self.s, self.other = nc, sets[turn], sets[1 - turn]

    def __enter__(self):
        self.block_guard = self.nc.Block()
        block = self.block_guard.__enter__()
        other = self.other

        @block.sync
        def _(sp):
            for n in other:
                sp.sem_clear(other[n])
        return block, self.s

    def __exit__(self, *exc):
        return self.block_guard.__exit__(*exc)


class Link:

    def __init__(self, eng, sem):
        self.eng, self.sem, self.n = eng, sem, 0

    def __call__(self, ins):
        ins.then_inc(self.sem, 1)
        self.n += 1
        return ins

    def wait(self):
        self.eng.wait_ge(self.sem, self.n)


def build(nc, a, out):
    with ExitStack() as ctx:
        def sb(name, *shape):
            return ctx.enter_context(nc.sbuf_tensor(name, [P, *shape], F32))

        H = sb("H", KT, T)
        Y = sb("Y", KT, T)
        U = sb("U", 15360)
        RAW = sb("RAW", T + 4)
        W = sb("W", 2, KT * P)
        CST = sb("CST", N_CST)
        MOD = sb("MOD", 24, 2)
        GAIN = sb("GAIN", KT, 2)
        NG = sb("NG", KT)
        CC = sb("CC", KT, 2)
        ADAB = sb("ADAB", 24)
        RKC = sb("RKC", N_RKC)
        RKU = sb("RKU", N_RKU)
        MU = sb("MU", 3, 5)
        RTU = sb("RTU", N_RTU)
        GDU = sb("GDU", 2 * N_GDU)
        GS = sb("GS", NCH, 4, 2, N_GS)
        GSU = RKU[:, 100:100 + NCH * 4 * N_GS].rearrange("p (c h d q) -> p c h d q", c=NCH, h=2, d=2)
        GP = sb("GP", 2, 8)
        ST = sb("ST", 3, 2 * NCH)
        FG = sb("FG", KT)
        SL = sb("SL", 8 * 512)
        XY = sb("XY", 2, 2, 2, P)
        QS = sb("QS", 4, P)
        SLOTS = [sb(f"SLOT{q}", 1024) for q in range(2)]
        KTOK = sb("KTOK", 512)
        STATE = sb("STATE", 512)
        SCS = [sb(f"SC{q}", 2, 2, N_GS) for q in range(2)]
        PS = [ctx.enter_context(nc.psum_tensor(f"PS{b}", [P, 512], F32)) for b in range(8)]
        x_next = nc.dram_tensor("x_next", (KT, P, T), F32, kind="Internal").ap()
        v_first = nc.dram_tensor("v_first", (2, P, T), F32, kind="Internal").ap()

        def cst(at, n=P):
            return CST[:, at:at + n]

        IDENT, ONES, BLK = cst(C_IDENT), cst(C_ONES), cst(C_BLK)
        YT = [Y[:, t, :] for t in range(KT)]

        def pieces(ps=0):
            return [(PS[ps + n], t0, m) for n, (t0, m) in enumerate(PIECES)]

        def chunked(tile):
            return tile.rearrange("p (c t) -> p c t", t=CH)

        def load_weights(sp, s, tile_of, n, layer):
            for j in range(n):
                if j >= 2:
                    sp.wait_ge(s["projected"], 3 * (j - 1))
                sp.dma_start(W[:, j % 2, :], a["w_t"][layer, bass.ds(tile_of + j, 1)].rearrange("a p n -> p (a n)")
                             ).then_inc(s[f"w_loaded{j % 2}"], 16)
            for q in range(2):
                sp.wait_ge(s[f"w_loaded{q}"], 16 * ((n - 1 - q) // 2 + 1))

        def project(pe, s, j):
            pe.wait_ge(s[f"w_loaded{j % 2}"], 16 * (j // 2 + 1))
            for n, (bank, t0, m) in enumerate(pieces()):
                if j:
                    pe.wait_ge(s["taken"], 3 * (j - 1) + n + 1)
                for k in range(KT):
                    mm = nc.tensor.matmul(bank[:, 0:m], W[:, j % 2, k * P:(k + 1) * P], H[:, k, t0:t0 + m],
                                          start=(k == 0), stop=(k == KT - 1))
                mm.then_inc(s["projected"], 1)

        def rsqrt_sum(act, s, link, bank, m, dst, scale, eps, after):
            link(nc.scalar.activation(dst, bank[:, 0:m], ACT.Ln, scale=scale, bias=eps))
            link.wait()
            nc.scalar.activation(dst, dst, ACT.Exp, scale=-0.5, bias=after)

        def column_sums(pe, tile, weights, ps=0):
            for bank, t0, m in pieces(ps):
                mm = nc.tensor.matmul(bank[:, 0:m], weights, tile[:, t0:t0 + m], start=True, stop=True)
            return mm

        EPSC = sb("EPSC", 4)
        HALF_LN = -0.5 * math.log(P)
        with Stage(nc, "loaded") as (block, s):
            @block.sync
            def _(sp):
                sp.dma_start(CST[:, :], a["consts"]).then_inc(s["loaded"], 16)
                sp.dma_start(CC[:, :, :], a["cc"]).then_inc(s["loaded"], 16)
                sp.dma_start(FG[:, :], a["final_g"]).then_inc(s["loaded"], 16)
                sp.dma_start(H[:, :, :], a["xT"].rearrange("k p t -> p k t")).then_inc(s["loaded"], 16)
                sp.wait_ge(s["loaded"], 64)

            @block.gpsimd
            def _(pool):
                nc.gpsimd.memset(RAW[:, :], 0.0)
                nc.gpsimd.memset(EPSC[:, 0:1], EPS)
                nc.gpsimd.memset(EPSC[:, 1:2], LN_EPS)
                nc.gpsimd.memset(EPSC[:, 2:3], HALF_LN)
                nc.gpsimd.memset(EPSC[:, 3:4], 1.0)

        with Stage(nc, "ready") as (block, s):
            @block.scalar
            def _(act):
                nc.scalar.activation(CC[:, :, :], CC[:, :, :], ACT.Silu)

        EPS_C, LNEPS_C, HALFLN_C, ONE_C = (EPSC[:, q:q + 1] for q in range(4))

        RSTD = U[:, 6144:6144 + T]
        SQ = [U[:, 6144 + T * (1 + q):6144 + T * (2 + q)] for q in range(2)]

        def mean_square_scalar(act, s):
            link = Link(act, s["act_order"])
            for k in range(KT):
                if k >= 2:
                    act.wait_ge(s["summed"], k - 1)
                nc.scalar.activation(SQ[k % 2], H[:, k, :], ACT.Square).then_inc(s["squared"], 1)
            act.wait_ge(s["summed"], KT)
            for bank, t0, m in pieces():
                link(nc.scalar.activation(RSTD[:, t0:t0 + m], bank[:, 0:m], ACT.Ln, scale=1.0 / D, bias=EPS_C))
            link.wait()
            nc.scalar.activation(RSTD, RSTD, ACT.Exp, scale=-0.5).then_inc(s["rstd_ready"], 1)

        def mean_square_tensor(pe, s):
            for k in range(KT):
                pe.wait_ge(s["squared"], k + 1)
                for bank, t0, m in pieces():
                    mm = nc.tensor.matmul(bank[:, 0:m], ONES, SQ[k % 2][:, t0:t0 + m], start=(k == 0), stop=(k == KT - 1))
                mm.then_inc(s["summed"], 1)

        def modulate(layer):
            AW = U[:, 0:2 * KT * 384].rearrange("p (b k n) -> p b k n", b=2, k=KT)
            MV = U[:, 6144 + 3 * T:6144 + 3 * T + 24 * P]
            with Stage(nc, "w_loaded0 w_loaded1 small_loaded multiplied row_taken turned order "
                           "squared summed rstd_ready act_order") as (block, s):
                @block.sync
                def _(sp):
                    for g in range(8):
                        if g >= 2:
                            sp.wait_ge(s["multiplied"], g - 1)
                        sp.dma_start(AW[:, g % 2], a["ada_w"][layer, g]).then_inc(s[f"w_loaded{g % 2}"], 16)
                        if g == 1:
                            sp.dma_start(ADAB[:, :], a["ada_b"][layer]).then_inc(s["small_loaded"], 16)
                            sp.dma_start(NG[:, :], a["norm_g"][layer]).then_inc(s["small_loaded"], 16)
                            sp.dma_start(RKC[:, :], a["rkc"][layer]).then_inc(s["small_loaded"], 16)
                            sp.dma_start(GP[:, :, :], a["gda"][layer]).then_inc(s["small_loaded"], 16)

                @block.tensor
                def _(pe):
                    mean_square_tensor(pe, s)
                    for g in range(9):
                        if g < 8:
                            pe.wait_ge(s[f"w_loaded{g % 2}"], 16 * (g // 2 + 1))
                            if g >= 2:
                                pe.wait_ge(s["row_taken"], g - 1)
                            for k in range(KT):
                                mm = nc.tensor.matmul(PS[3 + g % 2][0:2, 0:384], CC[:, k, :], AW[:, g % 2, k, :],
                                                      start=(k == 0), stop=(k == KT - 1))
                            mm.then_inc(s["multiplied"], 1)
                        if g:
                            pe.wait_ge(s["row_taken"], g)
                            for n in range(3 * (g - 1), 3 * g):
                                mm = nc.tensor.matmul(PS[5][:, 2 * n:2 * n + 2], MV[0:2, n * P:(n + 1) * P], IDENT[0:2, 0:2],
                                                      start=True, stop=True)
                            mm.then_inc(s["turned"], 1)

                @block.scalar
                def _(act):
                    mean_square_scalar(act, s)
                    for g in range(8):
                        act.wait_ge(s["multiplied"], g + 1)
                        nc.scalar.copy(MV[0:2, g * 384:(g + 1) * 384], PS[3 + g % 2][0:2, 0:384]).then_inc(s["row_taken"], 1)

                @block.vector
                def _(dve):
                    link = Link(dve, s["order"])
                    dve.wait_ge(s["rstd_ready"], 1)
                    for k in range(KT):
                        link(nc.vector.tensor_tensor(H[:, k, :], H[:, k, :], RSTD, ALU.mult))
                    dve.wait_ge(s["small_loaded"], 64)
                    dve.wait_ge(s["turned"], 8)
                    link(nc.vector.tensor_tensor(MOD[:, :, :], PS[5][:, 0:48].rearrange("p (n v) -> p n v", v=2),
                                                 ADAB[:, :, None].to_broadcast([P, 24, 2]), ALU.add))
                    link.wait()
                    link(nc.vector.tensor_scalar(GAIN[:, :, :], MOD[:, 8:16, :], 1.0, None, ALU.add))
                    link.wait()
                    link(nc.vector.tensor_tensor(GAIN[:, :, :], GAIN[:, :, :], NG[:, :, None].to_broadcast([P, KT, 2]), ALU.mult))
                    link.wait()
                    for k in range(KT):
                        for v, (t0, t1) in enumerate(((CTX, T), (0, CTX))):
                            nc.vector.tensor_scalar(H[:, k, t0:t1], H[:, k, t0:t1], GAIN[:, k, v:v + 1], MOD[:, k, v:v + 1],
                                                    ALU.mult, ALU.add)

        def mix(dve, link, dst, t, done):
            raw_c, raw_l = RAW[:, 1:1 + CTX], RAW[:, CTX + 3:CTX + 3 + SEQ]

            def coef(q):
                return MU[:, t, q:q + 1]

            def add(o, i, q):
                link.wait()
                link(nc.vector.scalar_tensor_tensor(o, i, coef(q), o, ALU.mult, ALU.add))

            link(nc.vector.tensor_scalar(dst[:, 0:CTX], raw_c, coef(0), None, ALU.mult))
            link(nc.vector.tensor_scalar(dst[:, CTX:T], raw_l, coef(0), None, ALU.mult))
            for q, back in ((1, True), (2, False), (3, True), (4, False)):
                if back:
                    add(dst[:, 1:CTX], raw_c[:, 0:CTX - 1], q)
                else:
                    add(dst[:, 0:CTX - 1], raw_c[:, 1:CTX], q)
            lat, src = dst[:, CTX:T].rearrange("p (r w) -> p r w", w=GRID), raw_l.rearrange("p (r w) -> p r w", w=GRID)
            add(lat[:, :, 1:GRID], src[:, :, 0:GRID - 1], 1)
            add(lat[:, :, 0:GRID - 1], src[:, :, 1:GRID], 2)
            add(dst[:, CTX + GRID:T], raw_l[:, 0:SEQ - GRID], 3)
            link.wait()
            nc.vector.scalar_tensor_tensor(dst[:, CTX:T - GRID], raw_l[:, GRID:SEQ], coef(4), dst[:, CTX:T - GRID],
                                           ALU.mult, ALU.add).then_inc(done, 1)

        def mu_columns(dve, link, src, n):
            link(nc.vector.tensor_scalar(MU[:, 0:n, 0], src, -1.0, 1.0, ALU.mult, ALU.add))
            for t in range(n):
                link(nc.vector.tensor_scalar(MU[:, t, 1:5], cst(C_TYPE, 4), src[:, t:t + 1], None, ALU.mult))
            link.wait()

        def raw_of(t0, m):
            return RAW[:, 1:1 + CTX] if t0 < CTX else RAW[:, t0 + 3:t0 + 3 + m]

        VT = [U[:, 0:T], U[:, T:2 * T]]
        WA = U[:, 2 * T:3 * T]
        VTOK = U[:, 3 * T:4 * T].rearrange("p (c n) -> p c n", c=NCH)
        PKG = U[:, 4 * T:12 * T].rearrange("p (d c f t) -> p d c f t", d=2, c=NCH, f=4)

        def rwkv_common(layer):
            with Stage(nc, "w_loaded0 w_loaded1 projected taken mixed act_order order stored vf_loaded "
                           "v1_done v1_taken v2_done v2_sig") as (block, s):
                dsts = [VT[0], VT[1], WA]

                @block.sync
                def _(sp):
                    load_weights(sp, s, W_RK_COMMON, 3, layer)
                    sp.wait_ge(s["mixed"], 3)
                    if layer == 0:
                        for q in range(2):
                            sp.dma_start(v_first[q], VT[q]).then_inc(s["stored"], 16)
                        sp.wait_ge(s["stored"], 32)
                    else:
                        for q in range(2):
                            sp.dma_start(YT[q], v_first[q]).then_inc(s["vf_loaded"], 16)

                @block.tensor
                def _(pe):
                    for j in range(3):
                        project(pe, s, j)
                    if layer:
                        pe.wait_ge(s["mixed"], 2)
                        for bank, t0, m in pieces(3):
                            for q in range(2):
                                mm = nc.tensor.matmul(bank[0:32, 0:m], RKC[:, RKC_V1 + 32 * q:RKC_V1 + 32 * (q + 1)],
                                                      VT[q][:, t0:t0 + m], start=(q == 0), stop=(q == 1))
                        mm.then_inc(s["v1_done"], 1)
                        pe.wait_ge(s["v1_taken"], 1)
                        for q in range(2):
                            if q:
                                pe.wait_ge(s["v2_sig"], 1)
                            for bank, t0, m in pieces(3):
                                mm = nc.tensor.matmul(bank[:, 0:m], RKC[0:32, RKC_V2 + P * q:RKC_V2 + P * (q + 1)],
                                                      YT[2][0:32, t0:t0 + m], start=True, stop=True)
                            mm.then_inc(s["v2_done"], 1)

                @block.scalar
                def _(act):
                    for j in range(3):
                        for n, (bank, t0, m) in enumerate(pieces()):
                            act.wait_ge(s["projected"], 3 * j + n + 1)
                            if j and n == 0:
                                act.wait_ge(s["mixed"], j)
                            nc.scalar.copy(raw_of(t0, m), bank[:, 0:m]).then_inc(s["taken"], 1)
                    act.wait_ge(s["mixed"], 3)
                    nc.scalar.activation(WA[0:64], WA[0:64], ACT.Tanh)
                    if layer:
                        act.wait_ge(s["v1_done"], 1)
                        for bank, t0, m in pieces(3):
                            ins = nc.scalar.copy(YT[2][0:32, t0:t0 + m], bank[0:32, 0:m])
                        ins.then_inc(s["v1_taken"], 1)
                        for q in range(2):
                            act.wait_ge(s["v2_done"], q + 1)
                            for bank, t0, m in pieces(3):
                                ins = nc.scalar.activation(YT[4 + q][:, t0:t0 + m], bank[:, 0:m], ACT.Sigmoid,
                                                           bias=RKC[:, RKC_V0 + q:RKC_V0 + q + 1])
                            ins.then_inc(s["v2_sig"], 1)

                @block.vector
                def _(dve):
                    link = Link(dve, s["order"])
                    mu_columns(dve, link, RKC[:, RKC_MU:RKC_MU + 3], 3)
                    for j in range(3):
                        dve.wait_ge(s["taken"], 3 * (j + 1))
                        mix(dve, link, dsts[j], j, s["mixed"])
                    if layer:
                        dve.wait_ge(s["vf_loaded"], 32)
                        for q in range(2):
                            link(nc.vector.tensor_tensor(YT[q], YT[q], VT[q], ALU.subtract))
                            dve.wait_ge(s["v2_sig"], q + 1)
                            link.wait()
                            link(nc.vector.tensor_tensor(YT[q], YT[q], YT[4 + q], ALU.mult))
                            link.wait()
                            link(nc.vector.tensor_tensor(VT[q], YT[q], VT[q], ALU.add))

        def rwkv_project(layer, p):
            with Stage(nc, "w_loaded0 w_loaded1 projected taken mixed order param_loaded v_copied "
                           "kk_squared kk_summed kk_ln kk_rstd turned") as (block, s):
                @block.sync
                def _(sp):
                    sp.dma_start(RKU[:, :], a["rku"][layer, bass.ds(p, 1)].rearrange("a q n -> q (a n)")
                                 ).then_inc(s["param_loaded"], 16)
                    load_weights(sp, s, W_RK + 3 * p, 3, layer)
                    sp.wait_ge(s["param_loaded"], 16)

                @block.tensor
                def _(pe):
                    for j in range(3):
                        project(pe, s, j)
                    pe.wait_ge(s["v_copied"], 1)
                    for c in range(NCH):
                        bank, col = (PS[3], c * P) if c < 2 else (PS[4 + (c - 2) // 4], (c - 2) % 4 * P)
                        tr = nc.tensor.transpose(bank[:, col:col + P], PT[:, c * P:(c + 1) * P], IDENT)
                    tr.then_inc(s["turned"], 1)
                    pe.wait_ge(s["kk_squared"], 1)
                    pe.wait_ge(s["taken"], 9)
                    column_sums(pe, L, BLK).then_inc(s["kk_summed"], 1)

                @block.scalar
                def _(act):
                    for j in range(2):
                        for n, (bank, t0, m) in enumerate(pieces()):
                            act.wait_ge(s["projected"], 3 * j + n + 1)
                            if j and n == 0:
                                act.wait_ge(s["mixed"], j)
                            nc.scalar.copy(raw_of(t0, m), bank[:, 0:m]).then_inc(s["taken"], 1)
                    for n, (bank, t0, m) in enumerate(pieces()):
                        act.wait_ge(s["projected"], 7 + n)
                        nc.scalar.activation(Y[:, bass.ds(p, 1), t0:t0 + m], bank[:, None, 0:m], ACT.Silu).then_inc(s["taken"], 1)
                    act.wait_ge(s["turned"], 1)
                    for bank, t0, m in pieces(3):
                        nc.scalar.copy(VTOK[:, t0 // P:(t0 + m) // P, :], bank[:, 0:m].rearrange("p (c n) -> p c n", n=P))
                    act.wait_ge(s["kk_summed"], 1)
                    for bank, t0, m in pieces():
                        ins = nc.scalar.activation(L[:, t0:t0 + m], bank[:, 0:m], ACT.Ln, bias=EPS_C)
                    ins.then_inc(s["kk_ln"], 1)
                    act.wait_ge(s["kk_ln"], 1)
                    nc.scalar.activation(L, L, ACT.Exp, scale=-0.5).then_inc(s["kk_rstd"], 1)

                @block.vector
                def _(dve):
                    link = Link(dve, s["order"])
                    nc.vector.tensor_copy(PT[:, None, :], U[:, 0:2 * T].rearrange("p (q t) -> p q t", q=2)[:, bass.ds(p, 1), :]
                                          ).then_inc(s["v_copied"], 1)
                    dve.wait_ge(s["param_loaded"], 16)
                    mu_columns(dve, link, RKU[:, RKU_MU:RKU_MU + 2], 2)
                    for j, dst in enumerate((R, K)):
                        dve.wait_ge(s["taken"], 3 * (j + 1))
                        mix(dve, link, dst, j, s["mixed"])
                    dve.wait_ge(s["mixed"], 2)
                    link(nc.vector.tensor_scalar(KK, K, RKU[:, RKU_KK:RKU_KK + 1], None, ALU.mult))
                    link.wait()
                    nc.vector.tensor_tensor(L, KK, KK, ALU.mult).then_inc(s["kk_squared"], 1)
                    dve.wait_ge(s["kk_rstd"], 1)
                    nc.vector.tensor_tensor(KK, KK, L, ALU.mult)

        R, K, KK, L, PT, IC = YT[2], YT[3], YT[4], YT[5], YT[6], YT[7]
        EC = sb("EC", 2, NCH + 1)

        def rwkv_packages(p, d):
            with Stage(nc, "lora_done decay_sig rate_sig log_ready exp_ready order bonus_ready bonus_summed rates_summed "
                           "rated") as (block, s):
                PA, PR, PK, PB = (PKG[:, d, :, f, :] for f in range(4))
                ic_f = PKG[:, 1, :, 3, :]

                @block.tensor
                def _(pe):
                    for q, ps in ((0, 0), (1, 3)):
                        for bank, t0, m in pieces(ps):
                            nc.tensor.matmul(bank[:, 0:m], RKU[:, (2 * q + d) * P:(2 * q + d + 1) * P],
                                             WA[:, t0:t0 + m], start=True, stop=True).then_inc(s["lora_done"], 1)
                    if d:
                        pe.wait_ge(s["decay_sig"], 1)
                        pe.wait_ge(s["bonus_ready"], 1)
                        column_sums(pe, RAW, BLK).then_inc(s["bonus_summed"], 1)

                @block.scalar
                def _(act):
                    for q, (dst, ps, col, sem) in enumerate(((L, 0, RKU_W0, "decay_sig"), (IC, 3, RKU_A0, "rate_sig"))):
                        for n, (bank, t0, m) in enumerate(pieces(ps)):
                            act.wait_ge(s["lora_done"], 3 * q + n + 1)
                            ins = nc.scalar.activation(dst[:, t0:t0 + m], bank[:, 0:m], ACT.Sigmoid, bias=RKU[:, col + d:col + d + 1])
                        ins.then_inc(s[sem], 1)
                    c = NEG_SQRT_E
                    excl = (PA, c) if d == 0 else (chunked(PT), -c)
                    incl = PT if d == 0 else L
                    act.wait_ge(s["log_ready"], 1)
                    nc.scalar.activation(PA, excl[0], ACT.Exp, scale=excl[1]).then_inc(s["exp_ready"], 1)
                    nc.scalar.activation(PR, chunked(incl), ACT.Exp, scale=c).then_inc(s["exp_ready"], 1)
                    if d:
                        act.wait_ge(s["bonus_summed"], 1)
                    nc.scalar.activation(RAW[:, 0:T], incl, ACT.Exp, scale=-c).then_inc(s["exp_ready"], 1)
                    nc.scalar.activation(EC[:, d, 0:NCH], EC[:, d, 0:NCH], ACT.Exp, scale=c)

                @block.gpsimd
                def _(pool):
                    if d:
                        nc.gpsimd.memset(SCO, 0.0)
                        nc.gpsimd.memset(RST, 0.0)
                        nc.gpsimd.memset(RSM, 0.0)
                        pool.wait_ge(s["rates_summed"], 1)
                    pool.wait_ge(s["rate_sig"], 1)
                    if d == 0:
                        nc.gpsimd.tensor_copy(ic_f, chunked(IC))
                    nc.gpsimd.tensor_tensor(PB, chunked(IC), chunked(KK), ALU.mult).then_inc(s["rated"], 1)

                @block.vector
                def _(dve):
                    link = Link(dve, s["order"])
                    link(nc.vector.memset(EC[:, d, NCH:NCH + 1], 1.0))
                    dve.wait_ge(s["decay_sig"], 1)
                    for c in range(NCH):
                        link(nc.vector.tensor_tensor_scan(PT[:, c * P:(c + 1) * P], ONES, L[:, c * P:(c + 1) * P], 0.0,
                                                          ALU.mult, ALU.add))
                    link.wait()
                    link(nc.vector.tensor_scalar(EC[:, d, 0:NCH], chunked(PT)[:, :, P - 1], 0.5, None, ALU.mult))
                    link.wait()
                    link(nc.vector.tensor_tensor(chunked(PT), chunked(PT), EC[:, d, 0:NCH, None].to_broadcast([P, NCH, P]),
                                                 ALU.subtract))
                    link.wait()
                    if d == 0:
                        nc.vector.tensor_tensor(PA, chunked(PT), chunked(L), ALU.subtract).then_inc(s["log_ready"], 1)
                    else:
                        nc.vector.tensor_tensor(L, L, PT, ALU.subtract).then_inc(s["log_ready"], 1)
                    dve.wait_ge(s["rate_sig"], 1)
                    if d:
                        nc.vector.tensor_tensor(chunked(RAW[:, 0:T]), ic_f, chunked(IC), ALU.add).then_inc(s["rates_summed"], 1)
                        dve.wait_ge(s["rates_summed"], 1)
                        link(nc.vector.tensor_scalar(RAW[:, 0:T], RAW[:, 0:T], -2.0, RKU[:, RKU_KA:RKU_KA + 1], ALU.add, ALU.mult))
                        link.wait()
                        link(nc.vector.scalar_tensor_tensor(RAW[:, 0:T], RAW[:, 0:T], 2.0, K, ALU.add, ALU.mult))
                        link.wait()
                        nc.vector.scalar_tensor_tensor(RAW[:, 0:T], R, RKU[:, RKU_RK:RKU_RK + 1], RAW[:, 0:T],
                                                       ALU.mult, ALU.mult).then_inc(s["bonus_ready"], 1)
                    link(nc.vector.tensor_scalar(PK, chunked(IC), -1.0, RKU[:, RKU_KA:RKU_KA + 1], ALU.add, ALU.mult))
                    link.wait()
                    link(nc.vector.scalar_tensor_tensor(PK, PK, 1.0, chunked(K), ALU.add, ALU.mult))
                    dve.wait_ge(s["exp_ready"], 1)
                    link(nc.vector.tensor_tensor(PA, PA, chunked(KK), ALU.mult))
                    dve.wait_ge(s["exp_ready"], 2)
                    link(nc.vector.tensor_tensor(PR, PR, chunked(R), ALU.mult))
                    if d:
                        dve.wait_ge(s["bonus_summed"], 1)
                        for bank, t0, m in pieces():
                            vp = U[:, 0:2 * T].rearrange("p (q t) -> p q t", q=2)[:, bass.ds(p, 1), t0:t0 + m]
                            link(nc.vector.tensor_tensor(vp, vp, bank[:, None, 0:m], ALU.mult))
                    dve.wait_ge(s["exp_ready"], 3)
                    link.wait()
                    nc.vector.tensor_tensor(PK, PK, chunked(RAW[:, 0:T]), ALU.mult)
                    dve.wait_ge(s["rated"], 1)
                    nc.vector.tensor_tensor(PB, PB, chunked(RAW[:, 0:T]), ALU.mult)

        def lvl(level, d):
            at = C_LVL + (level * 2 + d) * P
            return CST[:, at:at + P]

        SOLVER = "lu_done q_ready xy_done first_ready x_taken y_taken "

        def y_of(m):
            return XY[:, m // 2, 1, m % 2, :]

        def solve_tensor(pe, s, ut, ready):
            for lv in range(LEVELS):
                for d in range(2):
                    if lv == 0:
                        ready(d)
                    elif lv == 1:
                        pe.wait_ge(s["first_ready"], d + 1)
                    else:
                        pe.wait_ge(s["x_taken"], 2 * (lv - 2) + d + 1)
                    for h in range(2):
                        mm = nc.tensor.matmul(PS[d][:, h * P:(h + 1) * P], ut(2 * d + h), IDENT if lv == 0 else XY[:, d, 0, h, :],
                                              start=True, stop=True)
                    mm.then_inc(s["lu_done"], 1)
                if lv == 0:
                    continue
                for d in range(2):
                    pe.wait_ge(s["q_ready"], 2 * (lv - 1) + d + 1)
                    if lv > 1:
                        pe.wait_ge(s["y_taken"], 2 * (lv - 2) + d + 1)
                    if lv < LEVELS - 1:
                        for h in range(2):
                            nc.tensor.matmul(PS[2 + d][:, h * P:(h + 1) * P], XY[:, d, 1, h, :], QS[:, 2 * d + h, :],
                                             start=True, stop=True)
                    for h in range(2):
                        mm = nc.tensor.matmul(PS[2 + d][:, 256 + h * P:256 + (h + 1) * P], QS[:, 2 * d + h, :], XY[:, d, 1, h, :],
                                              start=True, stop=True)
                    mm.then_inc(s["xy_done"], 1)

        def solve_vector(dve, s, ut2, between):
            for lv in range(LEVELS):
                for d in range(2):
                    if lv == 0:
                        nc.vector.tensor_tensor(XY[:, d, 1], ut2(d), lvl(0, 1 - d)[:, None, :].to_broadcast([P, 2, P]), ALU.mult)
                    dve.wait_ge(s["lu_done"], 2 * lv + d + 1)
                    mask = lvl(lv, d)[:, None, :].to_broadcast([P, 2, P])
                    p = PS[d][:, 0:256].rearrange("p (h n) -> p h n", h=2)
                    if lv == 0:
                        nc.vector.tensor_tensor(XY[:, d, 0], p, mask, ALU.mult).then_inc(s["first_ready"], 1)
                    else:
                        nc.vector.tensor_tensor(QS[:, 2 * d:2 * d + 2, :], p, mask, ALU.mult).then_inc(s["q_ready"], 1)
                        between(lv, d)

        def solve_scalar(act, s):
            for lv in range(1, LEVELS):
                for d in range(2):
                    act.wait_ge(s["xy_done"], 2 * (lv - 1) + d + 1)
                    for x, sem in enumerate(("x_taken", "y_taken")):
                        if x or lv < LEVELS - 1:
                            nc.scalar.copy(XY[:, d, x], PS[2 + d][:, 256 * x:256 * x + 256].rearrange("p (h n) -> p h n", h=2)
                                           ).then_inc(s[sem], 1)

        SCO = SL[:, 0:2048].rearrange("p (m f n) -> p m f n", m=4, f=4)
        RSS = [slot[:, :].rearrange("p (d f t) -> p d f t", d=2, f=4) for slot in SLOTS]
        R1S = SL[:, 2048:2304].rearrange("p (d n) -> p d n", d=2)
        NZ = SL[:, 2304:2560].rearrange("p (d n) -> p d n", d=2)
        RSM = SL[:, 3072:4096].rearrange("p (d h f t) -> p d h f t", d=2, h=2, f=2)
        VS = SL[:, 2560:2816].rearrange("p (d n) -> p d n", d=2)
        SUM = R1S
        ECS = SL[:, 2816:2820].rearrange("p (d q) -> p d q", d=2)
        TK = KTOK[:, :].rearrange("p (d f n) -> p d f n", d=2, f=2)
        RST = STATE[:, 0:256].rearrange("p (d n) -> p d n", d=2)

        def at(c):
            return slice(c, c + 1) if isinstance(c, int) else bass.ds(c, 1)

        def rwkv_init():
            with Stage(nc, "order") as (block, s):
                @block.vector
                def _(dve):
                    nc.vector.tensor_copy(SCO[:, :, 2, :], IDENT[:, None, :].to_broadcast([P, 4, P]))

        RWKV_SEMS = SOLVER + "slots_ready padded v_ready scored masked turned turn_taken r1_done r1_taken z_done z_taken o_done kv_done sum order"

        def rwkv_block(sets, turn, prep, scan):
            RS, RO = RSS[turn], RSS[1 - turn]

            def own(b):
                return bass.AP(PS[b], 0, [[512, P], [256, 2], [192, 2], [1, 64]])

            with StepStage(nc, sets, turn) as (block, s):
                @block.scalar
                def _(act):
                    def slot(d):
                        nc.scalar.copy(RS[:, d:d + 1], PKG[:, d, at(prep[d])]).then_inc(s["slots_ready"], 1)

                    if prep:
                        slot(0)
                    if scan:
                        act.wait_ge(s["r1_done"], 1)
                        nc.scalar.copy(R1S.rearrange("p d (h n) -> p d h n", h=2), own(4)).then_inc(s["r1_taken"], 1)
                    if prep:
                        slot(1)
                    if scan:
                        act.wait_ge(s["z_done"], 1)
                        nc.scalar.activation(NZ.rearrange("p d (h n) -> p d h n", h=2), own(6), ACT.Copy, scale=-1.0
                                             ).then_inc(s["z_taken"], 1)
                        act.wait_ge(s["kv_done"], 1)
                        for d in range(2):
                            nc.scalar.copy(PKG[:, d, at(scan[d]), 0, :].rearrange("p c (h n) -> p (c h) n", h=2), own(5)[:, d])
                    if prep:
                        act.wait_ge(s["turned"], 1)
                        nc.scalar.copy(TK, PS[7][:, :].rearrange("p (d f n) -> p d f n", d=2, f=2)).then_inc(s["turn_taken"], 1)
                        solve_scalar(act, s)

                @block.gpsimd
                def _(pool):
                    if prep:
                        for d in range(2):
                            for h in range(2):
                                rows = slice(64 * h, 64 * h + 64)
                                ins = nc.gpsimd.tensor_copy(RSM[rows, d, h:h + 1].rearrange("p h f t -> p h (f t)"),
                                                            PKG[rows, d, at(prep[d]), 0:2, :].rearrange("p c f t -> p c (f t)"))
                            ins.then_inc(s["padded"], 1)

                @block.tensor
                def _(pe):
                    def scores(d):
                        pe.wait_ge(s["slots_ready"], d + 1)
                        pe.wait_ge(s["padded"], d + 1)
                        for h in range(2):
                            for f in range(2):
                                mm = nc.tensor.matmul(PS[2 * d + h][:, 256 * f:256 * f + 256], RS[:, d, 2 + f, :],
                                                      RSM[:, d, h].rearrange("p f t -> p (f t)"), start=True, stop=True)
                            mm.then_inc(s["scored"], 1)

                    if scan:
                        for m in range(4):
                            o, d = PS[4][:, m * P:(m + 1) * P], m // 2
                            nc.tensor.matmul(o, RO[:, d, 0, :], RST[:, d, :], start=True, stop=False)
                            if m % 2 == 0:
                                pe.wait_ge(s["v_ready"], d + 1)
                            mm = nc.tensor.matmul(o, SCO[:, m, 0, :], VS[:, d, :], start=False, stop=True)
                        mm.then_inc(s["r1_done"], 1)
                    if prep:
                        scores(0)
                    if scan:
                        pe.wait_ge(s["r1_taken"], 1)
                        for m in range(4):
                            mm = nc.tensor.matmul(PS[6][:, m * P:(m + 1) * P], y_of(m), R1S[:, m // 2, :], start=True, stop=True)
                        mm.then_inc(s["z_done"], 1)
                    if prep:
                        scores(1)
                    if scan:
                        pe.wait_ge(s["z_taken"], 1)
                        for m in range(4):
                            o, d = PS[5][:, m * P:(m + 1) * P], m // 2
                            nc.tensor.matmul(o, RO[:, d, 1, :], RST[:, d, :], start=True, stop=False)
                            nc.tensor.matmul(o, SCO[:, m, 1, :], VS[:, d, :], start=False, stop=False)
                            mm = nc.tensor.matmul(o, SCO[:, m, 3, :], NZ[:, d, :], start=False, stop=True)
                            if m % 2:
                                mm.then_inc(s["o_done"], 1)
                        for d in range(2):
                            o = PS[6][:, d * P:(d + 1) * P]
                            nc.tensor.matmul(o, TK[:, d, 0, :], VS[:, d, :], start=True, stop=False)
                            mm = nc.tensor.matmul(o, TK[:, d, 1, :], NZ[:, d, :], start=False, stop=True)
                        mm.then_inc(s["kv_done"], 1)
                    if prep:
                        for d in range(2):
                            for f in range(2):
                                mm = nc.tensor.transpose(PS[7][:, (2 * d + f) * P:(2 * d + f + 1) * P], RS[:, d, 2 + f, :], IDENT)
                        mm.then_inc(s["turned"], 1)
                        solve_tensor(pe, s, lambda m: SCO[:, m, 2, :], lambda d: pe.wait_ge(s["masked"], 2 * d + 2))

                @block.vector
                def _(dve):
                    link = Link(dve, s["order"])
                    if scan:
                        for d in range(2):
                            nc.vector.tensor_copy(VS[:, d:d + 1, :], VTOK[:, at(scan[d]), :]).then_inc(s["v_ready"], 1)
                        for d in range(2):
                            link(nc.vector.tensor_copy(ECS[:, d, 0:1], EC[:, d, at(scan[d])]))
                            link(nc.vector.tensor_copy(ECS[:, d, 1:2], EC[:, d, at(scan[2 + d])]))
                    if prep:
                        for m in range(4):
                            d = m // 2
                            dve.wait_ge(s["scored"], m + 1)
                            if scan:
                                dve.wait_ge(s["o_done"], d + 1)
                            mask = CST[:, C_SI + d * 256:C_SI + (d + 1) * 256].bitcast(I32)[:, None, :].to_broadcast([P, 2, 256])
                            nc.vector.copy_predicated(SCO[:, m].rearrange("p (q g) n -> p q (g n)", q=2), mask,
                                                      PS[m][:, :].rearrange("p (q n) -> p q n", q=2)).then_inc(s["masked"], 1)

                    def advance(part):
                        if part == 0:
                            dve.wait_ge(s["kv_done"], 1)
                            dve.wait_ge(s["z_done"], 1)
                            link(nc.vector.tensor_tensor(SUM, PS[6][:, 0:256].rearrange("p (d n) -> p d n", d=2),
                                                         BLK[:, None, :].to_broadcast([P, 2, P]), ALU.mult))
                        elif part == 1:
                            link.wait()
                            link(nc.vector.tensor_tensor(SUM, SUM, RST, ALU.add))
                        elif part == 2:
                            link.wait()
                            for d in range(2):
                                nc.vector.tensor_scalar(RST[:, d, :], SUM[:, d, :], ECS[:, d, 0:1], ECS[:, d, 1:2],
                                                        ALU.mult, ALU.mult)

                    def between(lv, d):
                        if scan and d:
                            advance(lv - 1)

                    if prep:
                        dve.wait_ge(s["masked"], 4)
                        solve_vector(dve, s, lambda d: SCO[:, 2 * d:2 * d + 2, 2, :], between)
                    else:
                        for part in range(3):
                            advance(part)

        def run_scans(block, names, init):
            fwd = list(range(NCH))
            bwd = list(range(NC_CTX - 1, -1, -1)) + list(range(NCH - 1, NC_CTX - 1, -1))

            def at_step(k):
                n = min(k + 1, NCH - 1)
                return fwd[k], bwd[k], fwd[n], bwd[n]

            def later(k, i):
                return fwd[k] + 2 * i, bwd[k] - 2 * i, fwd[k] + 1 + 2 * i, bwd[k] - 1 - 2 * i

            init()
            settle(nc)
            with ExitStack() as sem_ctx:
                sets = [{n: sem_ctx.enter_context(nc.semaphore(f"{n}_{q}")) for n in names.split()} for q in range(2)]
                block(sets, 0, at_step(0)[0:2], None)
                block(sets, 1, at_step(1)[0:2], at_step(0))
                block(sets, 0, at_step(2)[0:2], at_step(1))
                with nc.Fori(0, (NCH - 4) // 2) as i:
                    block(sets, 1, later(3, i)[0:2], later(2, i))
                    block(sets, 0, later(4, i)[0:2], later(3, i))
                block(sets, 1, at_step(NCH - 1)[0:2], at_step(NCH - 2))
                block(sets, 0, None, at_step(NCH - 1))
                with nc.Block() as last:
                    @last.sync
                    def _(sp):
                        for n in sets[0]:
                            sp.sem_clear(sets[0][n])

        def normalise_heads(block, s, o_f, o_b, o, sq, heads, centred, eps):
            width = o.shape[3]

            @block.vector
            def _(dve):
                link = Link(dve, s["order"])
                n = NCH * heads
                mean, var, scale = (ST[:, q, 0:n].rearrange("p (c h) -> p c h", h=heads) for q in range(3))

                def wide(st):
                    return st[:, :, :, None].to_broadcast([P, NCH, heads, width])

                if o_b is not None:
                    link(nc.vector.tensor_tensor(o, o_f, o_b, ALU.add))
                    link.wait()
                if centred:
                    link(nc.vector.tensor_reduce(mean, o, AX, ALU.add))
                    link.wait()
                    link(nc.vector.tensor_scalar(mean, mean, 1.0 / width, None, ALU.mult))
                    link.wait()
                    link(nc.vector.tensor_tensor(o, o, wide(mean), ALU.subtract))
                    link.wait()
                link(nc.vector.tensor_tensor(sq, o, o, ALU.mult))
                link.wait()
                nc.vector.tensor_reduce(var, sq, AX, ALU.add).then_inc(s["var_ready"], 1)
                dve.wait_ge(s["rstd_ready"], 2)
                nc.vector.tensor_tensor(o, o, wide(scale), ALU.mult).then_inc(s["o_ready"], 1)

            def rstd(act):
                n = NCH * heads
                act.wait_ge(s["var_ready"], 1)
                nc.scalar.activation(ST[:, 2, 0:n], ST[:, 1, 0:n], ACT.Ln, scale=1.0 / width, bias=eps).then_inc(s["rstd_ready"], 1)
                act.wait_ge(s["rstd_ready"], 1)
                nc.scalar.activation(ST[:, 2, 0:n], ST[:, 2, 0:n], ACT.Exp, scale=-0.5).then_inc(s["rstd_ready"], 1)

            return rstd

        def turn_outputs(pe, s, o, ps):
            for c in range(NCH):
                bank, col = (PS[ps], c * P) if c < 2 else (PS[ps + 1 + (c - 2) // 4], (c - 2) % 4 * P)
                tr = nc.tensor.transpose(bank[:, col:col + P], o[:, c, :], IDENT)
            tr.then_inc(s["turned"], 1)

        def rwkv_post(p):
            o = PKG[:, 0, :, 1, :]
            with Stage(nc, "var_ready rstd_ready o_ready turned order out_order") as (block, s):
                heads = lambda x: x.rearrange("p c (h n) -> p c h n", h=2)
                OC = chunked(YT[2])
                rstd = normalise_heads(block, s, heads(PKG[:, 0, :, 0, :]), heads(PKG[:, 1, :, 0, :]), heads(OC),
                                       heads(chunked(YT[3])), 2, True, LNEPS_C)

                @block.scalar
                def _(act):
                    rstd(act)

                @block.tensor
                def _(pe):
                    pe.wait_ge(s["o_ready"], 1)
                    turn_outputs(pe, s, OC, 0)

                @block.vector
                def _(dve):
                    link = Link(dve, s["out_order"])
                    dve.wait_ge(s["turned"], 1)
                    for bank, t0, m in pieces():
                        bonus = U[:, 0:2 * T].rearrange("p (q t) -> p q t", q=2)[:, bass.ds(p, 1), t0:t0 + m]
                        tmp, y = YT[3][:, t0:t0 + m], Y[:, bass.ds(p, 1), t0:t0 + m]
                        link(nc.vector.tensor_scalar(tmp, bank[:, 0:m], RKU[:, RKU_LNG:RKU_LNG + 1], RKU[:, RKU_LNB:RKU_LNB + 1],
                                                     ALU.mult, ALU.add))
                        link.wait()
                        link(nc.vector.tensor_tensor(tmp[:, None, :], tmp[:, None, :], bonus, ALU.add))
                        link.wait()
                        link(nc.vector.tensor_tensor(y, y, tmp[:, None, :], ALU.mult))

        RQ, RKK = U[:, 0:T], U[:, T:2 * T]
        RVT = U[:, 2 * T:3 * T].rearrange("p (c n) -> p c n", c=NCH)
        RKT = U[:, 3 * T:4 * T].rearrange("p (c n) -> p c n", c=NCH)
        V2 = U[:, 4 * T:6 * T].rearrange("p (c d n) -> p c d n", c=NCH, d=2)
        SST = U[:, 6 * T:8 * T].rearrange("p (c d n) -> p c d n", c=NCH, d=2)
        ROPE = U[:, 8 * T:8 * T + 2 * SEQ].rearrange("p (q t) -> p q t", q=2)
        RO = U[:, 10 * T:11 * T].rearrange("p (c n) -> p c n", c=NCH)
        QD = [YT[4], YT[5]]
        DSUM = SL[:, 0:256].rearrange("p (h n) -> p h n", h=2)
        SCR = SL[:, 256:768].rearrange("p (b h n) -> p b h n", b=2, h=2)
        DTMP = SL[:, 768:1280].rearrange("p (m n) -> p m n", m=4)
        QDEC = SL[:, 1280:1536].rearrange("p (d n) -> p d n", d=2)
        LG = SL[:, 1536:1542]
        KDEC = SL[:, 1542:1546]
        CDEC = SL[:, 1546:1548]
        LTMP = SL[:, 1548:1554]

        def ret_project(layer, p):
            dsts = (RQ, RKK, YT[6])
            with Stage(nc, "w_loaded0 w_loaded1 projected taken param_loaded lg_a lg_b lg_c lg "
                           "decays order turned1 turned2 turn_taken swapped swap_taken rotated") as (block, s):
                @block.sync
                def _(sp):
                    sp.dma_start(RTU[:, :], a["rtu"][layer, bass.ds(p, 1)].rearrange("a q n -> q (a n)")
                                 ).then_inc(s["param_loaded"], 16)
                    sp.dma_start(ROPE, a["rope"].rearrange("q p t -> p q t")).then_inc(s["param_loaded"], 16)
                    load_weights(sp, s, W_RT + 4 * p, 4, layer)
                    sp.wait_ge(s["param_loaded"], 32)

                @block.tensor
                def _(pe):
                    for j in range(4):
                        project(pe, s, j)
                    pe.wait_ge(s["taken"], 12)
                    for c in range(NCH):
                        bank, col = (PS[3], c * P) if c < 2 else (PS[4 + (c - 2) // 4], (c - 2) % 4 * P)
                        tr = nc.tensor.transpose(bank[:, col:col + P], YT[6][:, c * P:(c + 1) * P], IDENT)
                    tr.then_inc(s["turned1"], 1)
                    for j, tile in enumerate((RQ, RKK)):
                        if j:
                            pe.wait_ge(s["swap_taken"], 2)
                        for bank, t0, m in pieces()[1:]:
                            mm = nc.tensor.matmul(bank[:, 0:m], cst(C_PERM), tile[:, t0:t0 + m], start=True, stop=True)
                        mm.then_inc(s["swapped"], 1)
                    pe.wait_ge(s["rotated"], 2)
                    pe.wait_ge(s["turn_taken"], 1)
                    for c in range(NCH):
                        bank, col = (PS[3], c * P) if c < 2 else (PS[4 + (c - 2) // 4], (c - 2) % 4 * P)
                        tr = nc.tensor.transpose(bank[:, col:col + P], RKK[:, c * P:(c + 1) * P], IDENT)
                    tr.then_inc(s["turned2"], 1)

                @block.scalar
                def _(act):
                    for j in range(3):
                        for n, (bank, t0, m) in enumerate(pieces()):
                            act.wait_ge(s["projected"], 3 * j + n + 1)
                            nc.scalar.activation(dsts[j][:, t0:t0 + m], bank[:, 0:m], ACT.Copy,
                                                 scale=0.125 if j == 1 else 1.0).then_inc(s["taken"], 1)
                    for n, (bank, t0, m) in enumerate(pieces()):
                        act.wait_ge(s["projected"], 10 + n)
                        nc.scalar.activation(Y[:, bass.ds(2 + p, 1), t0:t0 + m], bank[:, None, 0:m], ACT.Silu
                                             ).then_inc(s["taken"], 1)
                    act.wait_ge(s["param_loaded"], 32)
                    nc.scalar.activation(LTMP, RTU[:, 0:6], ACT.Abs).then_inc(s["lg_a"], 1)
                    act.wait_ge(s["lg_a"], 1)
                    nc.scalar.activation(LTMP, LTMP, ACT.Exp, scale=-1.0).then_inc(s["lg_a"], 1)
                    act.wait_ge(s["lg_a"], 2)
                    nc.scalar.activation(LTMP, LTMP, ACT.Ln, bias=ONE_C).then_inc(s["lg_b"], 1)
                    act.wait_ge(s["lg"], 1)
                    for d in range(2):
                        for h in range(2):
                            m = 2 * d + h
                            nc.scalar.activation(DTMP[:, m, :], cst(C_REL + d * P), ACT.Exp, scale=LG[:, m:m + 1])
                            nc.scalar.activation(KDEC[:, m:m + 1], cst(C_POSC + d, 1), ACT.Exp, scale=LG[:, m:m + 1])
                        nc.scalar.activation(QDEC[:, d, :], cst(C_POSR + d * P), ACT.Exp, scale=LG[:, 4 + d:5 + d])
                    nc.scalar.activation(CDEC, LG[:, 4:6], ACT.Exp, scale=float(CH)).then_inc(s["decays"], 1)
                    for q, sem in enumerate(("turned1", "turned2")):
                        act.wait_ge(s[sem], 1)
                        for bank, t0, m in pieces(3):
                            ins = nc.scalar.copy((RVT, RKT)[q][:, t0 // P:(t0 + m) // P, :],
                                                 bank[:, 0:m].rearrange("p (c n) -> p c n", n=P))
                        ins.then_inc(s["turn_taken"], 1)

                @block.vector
                def _(dve):
                    link = Link(dve, s["order"])
                    dve.wait_ge(s["lg_b"], 1)
                    nc.vector.scalar_tensor_tensor(LG, RTU[:, 0:6], 0.0, LTMP, ALU.min, ALU.subtract).then_inc(s["lg"], 1)
                    for j, tile in enumerate((RQ, RKK)):
                        dve.wait_ge(s["swapped"], j + 1)
                        for bank, t0, m in pieces()[1:]:
                            z, at0 = tile[:, t0:t0 + m], t0 - CTX
                            if t0 > CTX:
                                link.wait()
                            elif j:
                                dve.wait_ge(s["rotated"], j)
                            nc.vector.tensor_tensor(YT[7][:, 0:m], bank[:, 0:m], ROPE[:, 1, at0:at0 + m], ALU.mult
                                                    ).then_inc(s["swap_taken"], 1)
                            link(nc.vector.tensor_tensor(z, z, ROPE[:, 0, at0:at0 + m], ALU.mult))
                            link.wait()
                            dve.wait_ge(s["swap_taken"], 2 * j + (1 if t0 == CTX else 2))
                            if t0 == CTX:
                                link(nc.vector.tensor_tensor(z, z, YT[7][:, 0:m], ALU.add))
                            else:
                                nc.vector.tensor_tensor(z, z, YT[7][:, 0:m], ALU.add).then_inc(s["rotated"], 1)
                    dve.wait_ge(s["decays"], 1)
                    for h in range(2):
                        for d in range(2):
                            link(nc.vector.tensor_tensor(DTMP[:, 2 * d + h, :], DTMP[:, 2 * d + h, :],
                                                         cst(C_SI + d * 256 + P), ALU.mult))
                        link.wait()
                        link(nc.vector.tensor_tensor(DSUM[:, h, :], DTMP[:, h, :], DTMP[:, 2 + h, :], ALU.add))
                    dve.wait_ge(s["rotated"], 2)
                    for d in range(2):
                        link(nc.vector.tensor_tensor(chunked(QD[d]), chunked(RQ), QDEC[:, d, None, :].to_broadcast([P, NCH, P]),
                                                     ALU.mult))
                    dve.wait_ge(s["turn_taken"], 1)
                    for d in range(2):
                        for h in range(2):
                            m, cols = 2 * d + h, slice(64 * h, 64 * h + 64)
                            link(nc.vector.tensor_scalar(V2[:, :, d, cols], RVT[:, :, cols], KDEC[:, m:m + 1], None, ALU.mult))

        def ret_states():
            entering = [[0, 1] + list(range(2, NCH)), [1, 0] + list(range(NCH - 1, 1, -1))]
            with Stage(nc, "kv_done kv_taken order") as (block, s):
                @block.tensor
                def _(pe):
                    for c in range(NCH):
                        if c >= 4:
                            pe.wait_ge(s["kv_taken"], c - 3)
                        nc.tensor.matmul(PS[c % 4][:, 0:256], RKT[:, c, :], V2[:, c].rearrange("p d n -> p (d n)"),
                                         start=True, stop=True).then_inc(s["kv_done"], 1)

                @block.vector
                def _(dve):
                    link = Link(dve, s["order"])
                    for c in range(NCH):
                        dve.wait_ge(s["kv_done"], c + 1)
                        nc.vector.tensor_tensor(V2[:, c], PS[c % 4][:, 0:256].rearrange("p (d n) -> p d n", d=2),
                                                BLK[:, None, :].to_broadcast([P, 2, P]), ALU.mult).then_inc(s["kv_taken"], 1)
                    for d in range(2):
                        link(nc.vector.memset(SST[:, entering[d][0], d, :], 0.0))
                    dve.wait_ge(s["kv_taken"], NCH)
                    for q in range(1, NCH):
                        for d in range(2):
                            c, before = entering[d][q], entering[d][q - 1]
                            dve.wait_ge(s["order"], 2 * q - 1 + d)
                            link(nc.vector.scalar_tensor_tensor(SST[:, c, d, :], SST[:, before, d, :], CDEC[:, d:d + 1],
                                                                V2[:, before, d, :], ALU.mult, ALU.add))

        def ret_outputs():
            with Stage(nc, "scored masked o_done o_taken") as (block, s):
                @block.tensor
                def _(pe):
                    for c in range(NCH + 1):
                        if c < NCH:
                            if c >= 2:
                                pe.wait_ge(s["masked"], c - 1)
                            for h in range(2):
                                rows = slice(64 * h, 64 * h + 64)
                                mm = nc.tensor.matmul(PS[2 * (c % 2) + h][:, 0:P], RKK[rows, c * P:(c + 1) * P],
                                                      RQ[rows, c * P:(c + 1) * P], start=True, stop=True)
                            mm.then_inc(s["scored"], 1)
                        if c:
                            n = c - 1
                            o = PS[4 + n % 2]
                            if n >= 2:
                                pe.wait_ge(s["o_taken"], n - 1)
                            pe.wait_ge(s["masked"], n + 1)
                            for h in range(2):
                                nc.tensor.matmul(o[:, 64 * h:64 * h + 64], SCR[:, n % 2, h, :],
                                                 RVT[:, n, 64 * h:64 * h + 64], start=(h == 0), stop=False,
                                                 skip_group_check=True)
                            for d in range(2):
                                mm = nc.tensor.matmul(o[:, 0:P], QD[d][:, n * P:(n + 1) * P], SST[:, n, d, :],
                                                      start=False, stop=(d == 1), skip_group_check=True)
                            mm.then_inc(s["o_done"], 1)

                @block.vector
                def _(dve):
                    for c in range(NCH):
                        dve.wait_ge(s["scored"], c + 1)
                        if c >= 2:
                            dve.wait_ge(s["o_done"], c - 1)
                        for h in range(2):
                            ins = nc.vector.tensor_tensor(SCR[:, c % 2, h], PS[2 * (c % 2) + h][:, 0:P], DSUM[:, h], ALU.mult)
                        ins.then_inc(s["masked"], 1)

                @block.scalar
                def _(act):
                    for c in range(NCH):
                        act.wait_ge(s["o_done"], c + 1)
                        nc.scalar.copy(RO[:, c, :], PS[4 + c % 2][:, 0:P]).then_inc(s["o_taken"], 1)

        def ret_post(p):
            with Stage(nc, "var_ready rstd_ready o_ready turned order") as (block, s):
                heads = lambda x: x.rearrange("p c (h n) -> p c h n", h=2)
                rstd = normalise_heads(block, s, None, None, heads(RO), heads(V2[:, :, 0, :]), 2, False, EPS_C)

                @block.scalar
                def _(act):
                    rstd(act)

                @block.tensor
                def _(pe):
                    pe.wait_ge(s["o_ready"], 1)
                    turn_outputs(pe, s, RO, 0)

                @block.vector
                def _(dve):
                    dve.wait_ge(s["turned"], 1)
                    for bank, t0, m in pieces():
                        y = Y[:, bass.ds(2 + p, 1), t0:t0 + m]
                        nc.vector.scalar_tensor_tensor(y, bank[:, None, 0:m], RTU[:, RTU_G:RTU_G + 1], y, ALU.mult, ALU.mult)

        def gdn_scalars(layer):
            ab = U[:, 0:NCH * 16].rearrange("p (c q k) -> p c q k", c=NCH, q=2)
            sp_in, mag, rest = (U[:, 200 + 80 * q:280 + 80 * q].rearrange("p (c k) -> p c k", c=NCH) for q in range(3))
            wab = W[:, 0, 0:KT * 16].rearrange("p (k n) -> p k n", k=KT)
            nea = GP[:, 0, :]
            rows = U[:, 1024:1024 + T]

            def gs(q):
                return GS[:, :, :, :, q].rearrange("p c h d -> p c (h d)")

            with Stage(nc, "w_loaded0 rows_done rows_taken projected x_ready steps act_steps g_ready summed order") as (block, s):
                @block.sync
                def _(sp):
                    sp.dma_start(wab, a["w_ab"][layer]).then_inc(s["w_loaded0"], 16)

                @block.tensor
                def _(pe):
                    pe.wait_ge(s["w_loaded0"], 16)
                    for n, (bank, t0, m) in enumerate(pieces(2)):
                        for k in range(KT):
                            mm = nc.tensor.matmul(bank[0:16, 0:m], wab[:, k, :], H[:, k, t0:t0 + m],
                                                  start=(k == 0), stop=(k == KT - 1))
                        mm.then_inc(s["rows_done"], 1)
                    for n, (_, t0, m) in enumerate(pieces()):
                        pe.wait_ge(s["rows_taken"], n + 1)
                        for c in range(t0 // P, (t0 + m) // P):
                            mm = nc.tensor.transpose(PS[0][:, c * 16:(c + 1) * 16], rows[0:16, c * P:(c + 1) * P], IDENT[0:16, 0:16])
                    mm.then_inc(s["projected"], 1)
                    pe.wait_ge(s["g_ready"], 1)
                    for d in range(2):
                        nc.tensor.matmul(PS[1][:, 80 * d:80 * d + 80], cst(C_SI + d * 256 + P), rest.rearrange("p c k -> p (c k)"),
                                         start=True, stop=True)
                    nc.tensor.matmul(PS[1][:, 160:240], ONES, rest.rearrange("p c k -> p (c k)"),
                                     start=True, stop=True).then_inc(s["summed"], 1)

                @block.scalar
                def _(act):
                    nc.scalar.activation(nea, nea, ACT.Exp).then_inc(s["act_steps"], 1)
                    for n, (bank, t0, m) in enumerate(pieces(2)):
                        act.wait_ge(s["rows_done"], n + 1)
                        nc.scalar.copy(rows[0:16, t0:t0 + m], bank[0:16, 0:m]).then_inc(s["rows_taken"], 1)
                    act.wait_ge(s["x_ready"], 1)
                    nc.scalar.activation(mag, sp_in, ACT.Abs).then_inc(s["act_steps"], 1)
                    act.wait_ge(s["act_steps"], 2)
                    nc.scalar.activation(mag, mag, ACT.Exp, scale=-1.0).then_inc(s["act_steps"], 1)
                    act.wait_ge(s["act_steps"], 3)
                    nc.scalar.activation(mag, mag, ACT.Ln, bias=ONE_C).then_inc(s["act_steps"], 1)
                    nc.scalar.activation(gs(G_BETA), ab[:, :, 1, :], ACT.Sigmoid)
                    act.wait_ge(s["steps"], 1)
                    nc.scalar.activation(gs(G_EG), gs(G_NGC), ACT.Exp, scale=-1.0).then_inc(s["act_steps"], 1)
                    nc.scalar.activation(gs(G_WK), gs(G_WK), ACT.Exp)
                    nc.scalar.activation(gs(G_CD), PS[1][:, 160:240].rearrange("p (c k) -> p c k", c=NCH), ACT.Exp)

                @block.vector
                def _(dve):
                    link = Link(dve, s["order"])
                    dve.wait_ge(s["projected"], 1)
                    link(nc.vector.tensor_copy(ab, PS[0][:, 0:160].rearrange("p (c q k) -> p c q k", c=NCH, q=2)))
                    link.wait()
                    nc.vector.tensor_tensor(sp_in, ab[:, :, 0, :], GP[:, 1, None, :].to_broadcast([P, NCH, 8]), ALU.add
                                            ).then_inc(s["x_ready"], 1)
                    dve.wait_ge(s["act_steps"], 4)
                    link(nc.vector.scalar_tensor_tensor(sp_in, sp_in, 0.0, mag, ALU.max, ALU.add))
                    link.wait()
                    link(nc.vector.tensor_tensor(sp_in, sp_in, nea[:, None, :].to_broadcast([P, NCH, 8]), ALU.mult))
                    link.wait()
                    nc.vector.tensor_scalar(rest, sp_in, -1.0, -104.0, ALU.mult, ALU.max).then_inc(s["g_ready"], 1)
                    dve.wait_ge(s["g_ready"], 1)
                    link(nc.vector.tensor_copy(gs(G_G), rest))
                    dve.wait_ge(s["summed"], 1)
                    for d in range(2):
                        mine = PS[1][:, 80 * d:80 * d + 80].rearrange("p (c h d) -> p c h d", c=NCH, d=2)[:, :, :, d]
                        link(nc.vector.tensor_scalar(GS[:, :, :, d, G_NGC], mine, -1.0, None, ALU.mult))
                    link.wait()
                    nc.vector.tensor_tensor(gs(G_WK), gs(G_NGC), PS[1][:, 160:240].rearrange("p (c k) -> p c k", c=NCH), ALU.add
                                            ).then_inc(s["steps"], 1)
                    dve.wait_ge(s["act_steps"], 5)
                    nc.vector.tensor_scalar(gs(G_NEG), gs(G_EG), -1.0, None, ALU.mult)

        KQ = U[:, 0:4 * T].rearrange("p (h q t) -> p h q t", h=2, q=2)
        GVT = U[:, 4 * T:6 * T].rearrange("p (c h n) -> p c h n", c=NCH, h=2)
        GO = U[:, 6 * T:10 * T].rearrange("p (d c h n) -> p d c h n", d=2, c=NCH, h=2)
        TMP = [U[:, (6 + q) * T:(7 + q) * T] for q in range(4)]

        def gdn_project(layer, u):
            dsts = [KQ[:, 0, 0, :], KQ[:, 1, 0, :], KQ[:, 0, 1, :], KQ[:, 1, 1, :], TMP[0], TMP[1]]
            with Stage(nc, "w_loaded0 w_loaded1 projected taken convolved param_loaded silu order pads "
                           "turned turn_taken squared summed ln_done rstd_ready scaled") as (block, s):
                @block.sync
                def _(sp):
                    sp.dma_start(GDU[:, :], a["gdu"][layer]).then_inc(s["param_loaded"], 16)
                    load_weights(sp, s, W_GD + 8 * u, 8, layer)
                    sp.wait_ge(s["param_loaded"], 16)

                @block.gpsimd
                def _(pool):
                    for col in (0, CTX + 1, CTX + 2, T + 3):
                        ins = nc.gpsimd.memset(RAW[:, col:col + 1], 0.0)
                    ins.then_inc(s["pads"], 1)

                @block.tensor
                def _(pe):
                    for j in range(8):
                        project(pe, s, j)
                    pe.wait_ge(s["silu"], 6)
                    for h in range(2):
                        if h:
                            pe.wait_ge(s["turn_taken"], 1)
                        for c in range(NCH):
                            bank, col = (PS[3], c * P) if c < 2 else (PS[4 + (c - 2) // 4], (c - 2) % 4 * P)
                            tr = nc.tensor.transpose(bank[:, col:col + P], TMP[h][:, c * P:(c + 1) * P], IDENT)
                        tr.then_inc(s["turned"], 1)
                    pe.wait_ge(s["taken"], 24)
                    for j in range(4):
                        pe.wait_ge(s["squared"], j + 1)
                        if j:
                            pe.wait_ge(s["ln_done"], j)
                        column_sums(pe, TMP[2 + j % 2], ONES).then_inc(s["summed"], 1)

                @block.scalar
                def _(act):
                    for j in range(8):
                        h = j % 2
                        for n, (bank, t0, m) in enumerate(pieces()):
                            act.wait_ge(s["projected"], 3 * j + n + 1)
                            if j < 6:
                                if n == 0 and j:
                                    act.wait_ge(s["convolved"], j)
                                if n == 0:
                                    act.wait_ge(s["pads"], 1)
                                nc.scalar.copy(raw_of(t0, m), bank[:, 0:m]).then_inc(s["taken"], 1)
                            else:
                                nc.scalar.activation(Y[:, bass.ds(4 + 2 * u + h, 1), t0:t0 + m], bank[:, None, 0:m], ACT.Silu
                                                     ).then_inc(s["taken"], 1)
                        if 1 <= j <= 6:
                            act.wait_ge(s["convolved"], j)
                            nc.scalar.activation(dsts[j - 1], dsts[j - 1], ACT.Silu).then_inc(s["silu"], 1)
                    for h in range(2):
                        act.wait_ge(s["turned"], h + 1)
                        for bank, t0, m in pieces(3):
                            ins = nc.scalar.copy(GVT[:, t0 // P:(t0 + m) // P, h, :], bank[:, 0:m].rearrange("p (c n) -> p c n", n=P))
                        ins.then_inc(s["turn_taken"], 1)
                    for j in range(4):
                        act.wait_ge(s["summed"], j + 1)
                        t = TMP[j % 2]
                        if j >= 2:
                            act.wait_ge(s["scaled"], j - 1)
                        for bank, t0, m in pieces():
                            ins = nc.scalar.activation(t[:, t0:t0 + m], bank[:, 0:m], ACT.Ln, bias=EPS_C)
                        ins.then_inc(s["ln_done"], 1)
                        act.wait_ge(s["ln_done"], j + 1)
                        if j < 2:
                            nc.scalar.activation(t, t, ACT.Exp, scale=-0.5).then_inc(s["rstd_ready"], 1)
                        else:
                            nc.scalar.activation(t, t, ACT.Exp, scale=-0.5, bias=HALFLN_C).then_inc(s["rstd_ready"], 1)

                @block.vector
                def _(dve):
                    link = Link(dve, s["order"])
                    dve.wait_ge(s["param_loaded"], 16)
                    cols = RKU[:, 0:18]
                    for j in range(6):
                        dve.wait_ge(s["taken"], 3 * (j + 1))

                        def tap(q):
                            return RKU[:, 3 * j + q:3 * j + q + 1]

                        if j == 0:
                            link(nc.vector.tensor_copy(cols[:, None, :], GDU[:, :].rearrange("p (u n) -> p u n", u=2)[:, bass.ds(u, 1), 0:18]))
                            link.wait()
                        ranges = ((0, CTX, 0), (CTX, T, CTX + 2))
                        for t0, t1, r in ranges:
                            link(nc.vector.tensor_scalar(dsts[j][:, t0:t1], RAW[:, r:r + t1 - t0], tap(0), None, ALU.mult))
                        for q in (1, 2):
                            link.wait()
                            for t0, t1, r in ranges:
                                ins = nc.vector.scalar_tensor_tensor(dsts[j][:, t0:t1], RAW[:, r + q:r + q + t1 - t0], tap(q),
                                                                     dsts[j][:, t0:t1], ALU.mult, ALU.add)
                                if q == 2 and t1 == T:
                                    ins.then_inc(s["convolved"], 1)
                                else:
                                    link(ins)
                    for j in range(6):
                        if j < 4:
                            dve.wait_ge(s["silu"], j + 1)
                            if j >= 2:
                                dve.wait_ge(s["summed"], j - 1)
                            nc.vector.tensor_tensor(TMP[2 + j % 2], dsts[j], dsts[j], ALU.mult).then_inc(s["squared"], 1)
                        if j >= 2:
                            dve.wait_ge(s["rstd_ready"], j - 1)
                            nc.vector.tensor_tensor(dsts[j - 2], dsts[j - 2], TMP[j % 2], ALU.mult).then_inc(s["scaled"], 1)

        GM, EM, ESM, UT, AT, VD, VN, VK = (SL[:, 512 * q:512 * (q + 1)].rearrange("p (m n) -> p m n", m=4) for q in range(8))
        OS = VD
        KQSS = [slot[:, :].rearrange("p (d h q n) -> p d h q n", d=2, h=2, q=2) for slot in SLOTS]
        KT4 = KTOK[:, :].rearrange("p (m n) -> p m n", m=4)
        GST = STATE[:, :].rearrange("p (m n) -> p m n", m=4)

        def gdn_init(u):
            def init():
                with Stage(nc, "order") as (block, s):
                    @block.vector
                    def _(dve):
                        nc.vector.memset(GST, 0.0)
                        nc.vector.tensor_copy(GSU[:, :, :, :, :].rearrange("p c h d q -> p c (h d q)"),
                                              GS[:, :, bass.ds(2 * u, 2), :, :].rearrange("p c h d q -> p c (h d q)"))
            return init

        GDN_SEMS = SOLVER + ("slots_ready gm_ready gated clamped decayed es_ready em_ready ut_raw ut_ready at_ready scored turned "
                             "turn_taken ks_done vd_ready w_done vn_ready vk_ready os_ready av_done kv_done order")

        def gdn_block(sets, turn, prep, scan):
            KQS, KQO = KQSS[turn], KQSS[1 - turn]
            SC, SCO_ = SCS[turn], SCS[1 - turn]

            def col(t, m, q):
                return t[:, m // 2, m % 2, q:q + 1]

            def wide(t, q):
                return t[:, :, :, q:q + 1].rearrange("p d h q -> p (d h) q").to_broadcast([P, 4, P])

            def bank4(b):
                return PS[b][:, :].rearrange("p (m n) -> p m n", m=4)

            with StepStage(nc, sets, turn) as (block, s):
                @block.scalar
                def _(act):
                    if prep:
                        for d in range(2):
                            nc.scalar.copy(KQS[:, d].rearrange("p h q n -> p (h q) n"),
                                           KQ[:, :, :, bass.ds(prep[d] * P, P)].rearrange("p h q t -> p (h q) t")
                                           ).then_inc(s["slots_ready"], 1)
                        act.wait_ge(s["clamped"], 1)
                        nc.scalar.activation(EM, EM, ACT.Exp).then_inc(s["decayed"], 1)
                    if scan:
                        act.wait_ge(s["vn_ready"], 1)
                        for m in range(4):
                            ins = nc.scalar.activation(VK[:, m, :], VN[:, m, :], ACT.Copy, scale=col(SCO_, m, G_WK))
                        ins.then_inc(s["vk_ready"], 1)
                    if prep:
                        act.wait_ge(s["turned"], 1)
                        if scan:
                            act.wait_ge(s["kv_done"], 1)
                        nc.scalar.copy(KT4, bank4(3)).then_inc(s["turn_taken"], 1)
                        solve_scalar(act, s)

                @block.gpsimd
                def _(pool):
                    if prep:
                        pool.wait_ge(s["decayed"], 1)
                        for d in range(2):
                            ins = nc.gpsimd.tensor_tensor(ESM[:, 2 * d:2 * d + 2, :], EM[:, 2 * d:2 * d + 2, :],
                                                          CST[:, None, C_SI + d * 256:C_SI + d * 256 + P].to_broadcast([P, 2, P]),
                                                          ALU.mult)
                            ins.then_inc(s["es_ready"], 1)
                        pool.wait_ge(s["es_ready"], 2)
                        nc.gpsimd.tensor_tensor(EM, ESM, IDENT[:, None, :].to_broadcast([P, 4, P]), ALU.add).then_inc(s["em_ready"], 1)

                @block.tensor
                def _(pe):
                    def state_products(q):
                        for m in range(4):
                            mm = nc.tensor.matmul(PS[4 + q][:, m * P:(m + 1) * P], KQO[:, m // 2, m % 2, q, :], GST[:, m, :],
                                                  start=True, stop=True)
                        mm.then_inc(s["ks_done"], 1)

                    def scores(d):
                        pe.wait_ge(s["slots_ready"], d + 1)
                        for h in range(2):
                            mm = nc.tensor.matmul(PS[d][:, 256 * h:256 * h + 256], KQS[:, d, h, 0, :],
                                                  KQS[:, d, h, :, :].rearrange("p q n -> p (q n)"), start=True, stop=True)
                        mm.then_inc(s["scored"], 1)

                    if scan:
                        state_products(0)
                    if prep:
                        scores(0)
                        pe.wait_ge(s["gm_ready"], 1)
                        nc.tensor.matmul(PS[2][:, :], ONES, GM.rearrange("p m n -> p (m n)"), start=True, stop=True
                                         ).then_inc(s["gated"], 1)
                        scores(1)
                    if scan:
                        pe.wait_ge(s["vd_ready"], 1)
                        for m in range(4):
                            mm = nc.tensor.matmul(PS[6][:, m * P:(m + 1) * P], y_of(m), VD[:, m, :], start=True, stop=True)
                        mm.then_inc(s["w_done"], 1)
                        state_products(1)
                    if prep:
                        for m in range(4):
                            mm = nc.tensor.transpose(PS[3][:, m * P:(m + 1) * P], KQS[:, m // 2, m % 2, 0, :], IDENT)
                        mm.then_inc(s["turned"], 1)
                    if scan:
                        pe.wait_ge(s["vn_ready"], 1)
                        for m in range(4):
                            mm = nc.tensor.matmul(PS[7][:, m * P:(m + 1) * P], AT[:, m, :], VN[:, m, :], start=True, stop=True)
                        mm.then_inc(s["av_done"], 1)
                        pe.wait_ge(s["vk_ready"], 1)
                        for m in range(4):
                            mm = nc.tensor.matmul(PS[4][:, m * P:(m + 1) * P], KT4[:, m, :], VK[:, m, :], start=True, stop=True)
                        mm.then_inc(s["kv_done"], 1)
                    if prep:
                        pe.wait_ge(s["turn_taken"], 1)
                        pe.wait_ge(s["at_ready"], 1)
                        solve_tensor(pe, s, lambda m: UT[:, m, :], lambda d: pe.wait_ge(s["ut_ready"], 1))

                @block.vector
                def _(dve):
                    link = Link(dve, s["order"])
                    if prep:
                        for d in range(2):
                            link(nc.vector.tensor_copy(SC[:, d:d + 1], GSU[:, at(prep[d]), :, d, :]))
                        link.wait()
                        for m in range(4):
                            ins = nc.vector.tensor_scalar(GM[:, m, :], cst(C_SI + (m // 2) * 256 + P), col(SC, m, G_G), None, ALU.mult)
                        ins.then_inc(s["gm_ready"], 1)
                    if scan:
                        dve.wait_ge(s["ks_done"], 1)
                        for m in range(4):
                            v = GVT[:, at(scan[m // 2]), m % 2, :]
                            ins = nc.vector.scalar_tensor_tensor(VD[:, m:m + 1, :], PS[4][:, None, m * P:(m + 1) * P],
                                                                 col(SCO_, m, G_NEG), v, ALU.mult, ALU.add)
                        ins.then_inc(s["vd_ready"], 1)
                    if prep:
                        dve.wait_ge(s["gated"], 1)
                        for m in range(4):
                            ins = nc.vector.tensor_scalar(EM[:, m, :], PS[2][:, m * P:(m + 1) * P], col(SC, m, G_NGC), 0.0,
                                                          ALU.add, ALU.min)
                        ins.then_inc(s["clamped"], 1)
                    if scan:
                        dve.wait_ge(s["w_done"], 1)
                        nc.vector.tensor_tensor(VN, bank4(6), wide(SCO_, G_BETA), ALU.mult).then_inc(s["vn_ready"], 1)
                    if prep:
                        dve.wait_ge(s["scored"], 2)
                        for m in range(4):
                            b = PS[m // 2][:, 256 * (m % 2):256 * (m % 2) + P]
                            dve.wait_ge(s["es_ready"], m // 2 + 1)
                            ins = nc.vector.scalar_tensor_tensor(UT[:, m, :], b, col(SC, m, G_BETA), ESM[:, m, :], ALU.mult, ALU.mult)
                        ins.then_inc(s["ut_raw"], 1)
                        dve.wait_ge(s["ut_raw"], 1)
                        nc.vector.tensor_tensor(UT, UT, IDENT[:, None, :].to_broadcast([P, 4, P]), ALU.add).then_inc(s["ut_ready"], 1)
                        dve.wait_ge(s["em_ready"], 1)
                        if scan:
                            dve.wait_ge(s["av_done"], 1)
                        for d in range(2):
                            ins = nc.vector.tensor_tensor(AT[:, 2 * d:2 * d + 2, :],
                                                          PS[d][:, :].rearrange("p (h q n) -> p h q n", h=2, q=2)[:, :, 1, :],
                                                          EM[:, 2 * d:2 * d + 2, :], ALU.mult)
                        ins.then_inc(s["at_ready"], 1)

                    def output(part):
                        if part == 0:
                            dve.wait_ge(s["ks_done"], 2)
                            dve.wait_ge(s["w_done"], 1)
                            nc.vector.tensor_tensor(OS, bank4(5), wide(SCO_, G_EG), ALU.mult).then_inc(s["os_ready"], 1)
                            dve.wait_ge(s["av_done"], 1)
                            dve.wait_ge(s["os_ready"], 1)
                        nc.vector.tensor_tensor(GO[:, part, at(scan[part])].rearrange("p c h n -> p c (h n)"),
                                                PS[7][:, None, 256 * part:256 * part + 256],
                                                OS[:, 2 * part:2 * part + 2, :].rearrange("p (o h) n -> p o (h n)", o=1), ALU.add)

                    def advance(m):
                        if m == 0:
                            dve.wait_ge(s["kv_done"], 1)
                        nc.vector.scalar_tensor_tensor(GST[:, m, :], GST[:, m, :], col(SCO_, m, G_CD), PS[4][:, m * P:(m + 1) * P],
                                                       ALU.mult, ALU.add)

                    def between(lv, d):
                        if scan and d and lv <= 2:
                            advance(2 * lv - 2)
                            advance(2 * lv - 1)
                        elif scan and d and lv <= 4:
                            output(lv - 3)

                    if prep:
                        dve.wait_ge(s["ut_ready"], 1)
                        solve_vector(dve, s, lambda d: UT[:, 2 * d:2 * d + 2, :], between)
                    else:
                        for m in range(4):
                            advance(m)
                        for part in range(2):
                            output(part)

        def gdn_post(u):
            o = GO[:, 0]
            with Stage(nc, "var_ready rstd_ready o_ready turned order") as (block, s):
                rstd = normalise_heads(block, s, o, GO[:, 1], o, KQ[:, 0].rearrange("p q (c n) -> p c q n", n=P), 2, False, EPS_C)

                @block.scalar
                def _(act):
                    rstd(act)

                @block.tensor
                def _(pe):
                    pe.wait_ge(s["o_ready"], 1)
                    for h in range(2):
                        turn_outputs(pe, s, GO[:, 0, :, h, :], 3 * h)

                @block.vector
                def _(dve):
                    for h in range(2):
                        dve.wait_ge(s["turned"], h + 1)
                        for bank, t0, m in pieces(3 * h):
                            y = Y[:, bass.ds(4 + 2 * u + h, 1), t0:t0 + m]
                            nc.vector.scalar_tensor_tensor(y, bank[:, None, 0:m], GDU[:, GDU_G:GDU_G + 1], y, ALU.mult, ALU.mult)

        def project_out(layer, last):
            src = a["xT"] if layer == 0 else x_next
            part = pieces()[1:] if last else pieces()
            with nc.Fori(0, KT // 2) as i:
                with Stage(nc, "w_loaded0 w_loaded1 x_loaded0 x_loaded1 projected summed stored") as (block, s):
                    XO = [U[:, 0:T], U[:, T:2 * T]]

                    @block.sync
                    def _(sp):
                        for q in range(2):
                            sp.dma_start(W[:, q, :], a["w_o"][layer, bass.ds(2 * i + q, 1)].rearrange("a p n -> p (a n)")
                                         ).then_inc(s[f"w_loaded{q}"], 16)
                            sp.dma_start(XO[q], src[bass.ds(2 * i + q, 1)].rearrange("a p t -> p (a t)")).then_inc(s[f"x_loaded{q}"], 16)
                        sp.wait_ge(s["w_loaded0"], 16)
                        sp.wait_ge(s["x_loaded0"], 16)
                        if not last:
                            for q in range(2):
                                sp.wait_ge(s["summed"], len(part) * (q + 1))
                                sp.dma_start(x_next[bass.ds(2 * i + q, 1)].rearrange("a p t -> p (a t)"), XO[q]).then_inc(s["stored"], 16)
                            sp.wait_ge(s["stored"], 32)

                    @block.tensor
                    def _(pe):
                        for q in range(2):
                            pe.wait_ge(s[f"w_loaded{q}"], 16)
                            for n, (_, t0, m) in enumerate(part):
                                bank = PS[3 * q + n]
                                for k in range(KT):
                                    mm = nc.tensor.matmul(bank[:, 0:m], W[:, q, k * P:(k + 1) * P], Y[:, k, t0:t0 + m],
                                                          start=(k == 0), stop=(k == KT - 1))
                                mm.then_inc(s["projected"], 1)

                    @block.vector
                    def _(dve):
                        for q in range(2):
                            dve.wait_ge(s[f"x_loaded{q}"], 16)
                            for n, (_, t0, m) in enumerate(part):
                                v = 1 if t0 < CTX else 0
                                dve.wait_ge(s["projected"], len(part) * q + n + 1)
                                x = XO[q][:, t0:t0 + m]
                                nc.vector.scalar_tensor_tensor(x[:, None, :], PS[3 * q + n][:, None, 0:m],
                                                               MOD[:, bass.ds(16 + 2 * i + q, 1), v], x[:, None, :],
                                                               ALU.mult, ALU.add).then_inc(s["summed"], 1)

                    @block.scalar
                    def _(act):
                        for q in range(2):
                            act.wait_ge(s["summed"], len(part) * (q + 1))
                            t0 = part[0][1]
                            nc.scalar.copy(H[:, bass.ds(2 * i + q, 1), t0:T], XO[q][:, None, t0:T])
                settle(nc)

        for layer in range(DEPTH):
            modulate(layer)
            rwkv_common(layer)
            settle(nc)
            with nc.Fori(0, 2) as p:
                rwkv_project(layer, p)
                for d in range(2):
                    rwkv_packages(p, d)
                run_scans(rwkv_block, RWKV_SEMS, rwkv_init)
                rwkv_post(p)
                settle(nc)
            with nc.Fori(0, 2) as p:
                ret_project(layer, p)
                ret_states()
                ret_outputs()
                ret_post(p)
                settle(nc)
            gdn_scalars(layer)
            settle(nc)
            with nc.Fori(0, 2) as u:
                gdn_project(layer, u)
                run_scans(gdn_block, GDN_SEMS, gdn_init(u))
                gdn_post(u)
                settle(nc)
            project_out(layer, layer == DEPTH - 1)

        with Stage(nc, "squared summed rstd_ready act_order order ready stored") as (block, s):
            @block.scalar
            def _(act):
                mean_square_scalar(act, s)

            @block.tensor
            def _(pe):
                mean_square_tensor(pe, s)

            @block.vector
            def _(dve):
                dve.wait_ge(s["rstd_ready"], 1)
                for k in range(KT):
                    nc.vector.scalar_tensor_tensor(H[:, k, CTX:T], H[:, k, CTX:T], FG[:, k:k + 1], RSTD[:, CTX:T],
                                                   ALU.mult, ALU.mult).then_inc(s["ready"], 1)

            @block.sync
            def _(sp):
                for k in range(KT):
                    sp.wait_ge(s["ready"], k + 1)
                    sp.dma_start(out[k], H[:, k, CTX:T]).then_inc(s["stored"], 16)
                sp.wait_ge(s["stored"], 16 * KT)
        settle(nc)


def pack(x, c, ctx, c_ctx, ada_w, ada_b, norm_g, w_in, w_out, rk_mu, rk_w0, rk_w2, rk_a0, rk_a2, rk_kk, rk_ka, rk_rk,
         rk_v0, rk_v1, rk_v2, rk_ln_g, rk_ln_b, ret_decay, ret_norm_g, gdn_conv, gdn_a_log, gdn_dt_bias, gdn_norm_g, final_g):
    L = DEPTH

    def cols(v):
        return v.reshape(v.shape[0], -1, P).transpose(0, 2, 1)

    def tile(start):
        return list(range(start, start + P))

    order = [tile(512), tile(640), tile(768)]
    for p in range(2):
        order += [tile(128 * p), tile(256 + 128 * p), tile(896 + 128 * p)]
    for p in range(2):
        order += [tile(1152 + 256 * q + 128 * p) for q in range(4)]
    for u in range(2):
        order += [tile(2176 + 512 * q + 128 * (2 * u + h)) for q in (1, 0, 2, 3) for h in range(2)]
    order = np.array(order)
    w = w_in.reshape(L, KT, P, N_IN)
    w_t = w[:, :, :, order.ravel()].reshape(L, KT, P, N_WT, P).transpose(0, 3, 2, 1, 4).reshape(L, N_WT, P, KT * P)
    ab = np.array([4224 + 8 * kind + 4 * d + h for kind in range(2) for h in range(4) for d in range(2)])
    w_ab = w[:, :, :, ab].transpose(0, 2, 1, 3)
    rkc = np.zeros((L, P, N_RKC), np.float32)
    rkc[:, :, 0:3] = cols(rk_mu)[:, :, 4:7]
    rkc[1:, :, RKC_V0:RKC_V1] = cols(rk_v0)
    rkc[1:, :, RKC_V1:RKC_V2] = rk_v1.reshape(L - 1, 2, P, 32).transpose(0, 2, 1, 3).reshape(L - 1, P, 64)
    rkc[1:, 0:32, RKC_V2:N_RKC] = rk_v2
    rku = np.zeros((L, 2, P, N_RKU), np.float32)
    rku[:, :, 0:64, 0:256] = rk_w2.reshape(L, 2, 64, 2, P).transpose(0, 3, 2, 1, 4).reshape(L, 2, 64, 256)
    rku[:, :, 64:128, 256:512] = rk_a2.reshape(L, 2, 64, 2, P).transpose(0, 3, 2, 1, 4).reshape(L, 2, 64, 256)
    rku[:, :, :, RKU_W0:RKU_A0] = rk_w0.reshape(L, 2, 2, P).transpose(0, 2, 3, 1)
    rku[:, :, :, RKU_A0:RKU_KK] = rk_a0.reshape(L, 2, 2, P).transpose(0, 2, 3, 1)
    for at, v in ((RKU_KK, rk_kk), (RKU_KA, rk_ka), (RKU_RK, rk_rk.reshape(L, -1)), (RKU_LNG, rk_ln_g), (RKU_LNB, rk_ln_b),
                  (RKU_MU, rk_mu[:, 0:256]), (RKU_MU + 1, rk_mu[:, 256:512])):
        rku[:, :, :, at] = v.reshape(L, 2, P)
    rtu = np.zeros((L, 2, P, N_RTU), np.float32)
    by_pair = ret_decay.reshape(L, 2, 2, 2)
    rtu[:, :, :, 0:4] = by_pair.transpose(0, 2, 1, 3).reshape(L, 2, 1, 4)
    rtu[:, :, :, 4:6] = np.repeat(by_pair.transpose(0, 2, 3, 1), 64, axis=2)
    rtu[:, :, :, RTU_G] = ret_norm_g.reshape(L, 2, P)
    conv = gdn_conv.reshape(L, 3, 3, 4, P)
    gdu = np.zeros((L, P, 2, N_GDU), np.float32)
    for u in range(2):
        for j, q in enumerate((1, 0, 2)):
            for h in range(2):
                gdu[:, :, u, 3 * (2 * j + h):3 * (2 * j + h) + 3] = conv[:, :, q, 2 * u + h, :].transpose(0, 2, 1)
        gdu[:, :, u, GDU_G] = gdn_norm_g
    gda = np.stack([gdn_a_log.transpose(0, 2, 1).reshape(L, 8), gdn_dt_bias.transpose(0, 2, 1).reshape(L, 8)], 1)
    out = {
        "xT": np.concatenate([ctx[0], x[0]], 0).T.reshape(KT, P, T),
        "cc": np.stack([c[0], c_ctx], -1).reshape(KT, P, 2).transpose(1, 0, 2),
        "ada_w": ada_w.reshape(L, KT, P, 8, 384).transpose(0, 3, 2, 1, 4),
        "ada_b": cols(ada_b), "norm_g": cols(norm_g), "final_g": cols(final_g[None])[0],
        "w_t": w_t, "w_ab": w_ab,
        "w_o": w_out.reshape(L, KT, P, KT, P).transpose(0, 3, 2, 1, 4).reshape(L, KT, P, KT * P),
        "rkc": rkc, "rku": rku, "rtu": rtu, "gdu": gdu.reshape(L, P, 2 * N_GDU),
        "gda": np.broadcast_to(gda[:, None], (L, P, 2, 8)),
        "consts": constants(), "rope": rope_tables(),
    }
    return {k: np.ascontiguousarray(v) for k, v in out.items()}


def kernel(**inputs):
    import concourse.bacc as bacc
    from concourse.bass_utils import run_bass_kernel_spmd

    nc = bacc.Bacc("TRN2", target_bir_lowering=False, num_devices=1)
    arrays = pack(**{k: np.asarray(v) for k, v in inputs.items()})
    aps = {k: nc.dram_tensor(k + "_in", v.shape, F32, kind="ExternalInput").ap() for k, v in arrays.items()}
    out = nc.dram_tensor("latents_out", (KT, P, SEQ), F32, kind="ExternalOutput").ap()
    build(nc, aps, out)
    r = run_bass_kernel_spmd(nc, [{k + "_in": v for k, v in arrays.items()}], core_ids=[0])
    return r.results[0]["latents_out"].reshape(1, D, SEQ).transpose(0, 2, 1)
```
